# Optimizing a Trainium2 kernel written in Bass

```python
import jax
import jax.numpy as jnp
from jax import lax
import numpy as np

D_MODEL = 1024
BATCH = 1
SEQ = 256
DEPTH = 4

N_MIXERS = 3
EPS = 1e-6
D_FF = 2816
A_HEADS = 16
A_KV_HEADS = 4
A_HEAD_DIM = D_MODEL // A_HEADS
A_WINDOW = 128
A_BLOCK = 128
A_ROPE_DIM = A_HEAD_DIM // 4
ROPE_THETA = 500000.0
M_HEADS = 8
M_QK_DIM = D_MODEL // (2 * M_HEADS)
M_V_DIM = D_MODEL // M_HEADS
M_CHUNK = 64
M_GATE_CAP = 15.0
R_HEADS = 4
R_QK_DIM = D_MODEL // R_HEADS
R_V_DIM = 2 * D_MODEL // R_HEADS
R_CHUNK = 128
R_THETA = 10000.0
N_ATTN = (DEPTH + 2) // N_MIXERS
N_MLSTM = (DEPTH + 1) // N_MIXERS
N_RET = DEPTH // N_MIXERS
A_QKV_DIM = (A_HEADS + 2 * A_KV_HEADS) * A_HEAD_DIM
M_IN_DIM = 2 * M_HEADS * M_QK_DIM + 2 * M_HEADS * M_V_DIM + 2 * M_HEADS
R_IN_DIM = 2 * R_HEADS * R_QK_DIM + 2 * R_HEADS * R_V_DIM

kernel_name = 'hybrid_swa_mlstm_retention_macaron'

def rms_norm(x, w):
    xf = x.astype(jnp.float32)
    y = xf * lax.rsqrt(jnp.mean(xf * xf, axis=-1, keepdims=True) + EPS)
    return (y * w.astype(jnp.float32)).astype(x.dtype)

def swiglu(x, w_in, w_out):
    gate, up = jnp.split(x @ w_in, 2, axis=-1)
    return (jax.nn.silu(gate) * up) @ w_out

def partial_rope(x, pos, rot_dim, theta):
    inv = 1.0 / (theta ** (jnp.arange(0, rot_dim, 2, dtype=jnp.float32) / rot_dim))
    ang = pos.astype(jnp.float32)[:, :, None, None] * inv
    cos, sin = jnp.cos(ang), jnp.sin(ang)
    xf = x.astype(jnp.float32)
    half = rot_dim // 2
    x1, x2, rest = xf[..., :half], xf[..., half:rot_dim], xf[..., rot_dim:]
    return jnp.concatenate([x1 * cos - x2 * sin, x2 * cos + x1 * sin, rest], axis=-1).astype(x.dtype)

def retnet_rotate(x, pos, theta):
    d = x.shape[-1]
    inv = 1.0 / (theta ** jnp.linspace(0.0, 1.0, d // 2, dtype=jnp.float32))
    ang = pos.astype(jnp.float32)[:, :, None, None] * inv
    cos, sin = jnp.cos(ang), jnp.sin(ang)
    xf = x.astype(jnp.float32)
    x1, x2 = xf[..., 0::2], xf[..., 1::2]
    return jnp.stack([x1 * cos - x2 * sin, x2 * cos + x1 * sin], axis=-1).reshape(x.shape).astype(x.dtype)

def swa_sink_attention(h, pos, w_qkv, b_qkv, w_o, b_o, sinks):
    B, S, _ = h.shape
    L, KV, G, hd = A_BLOCK, A_KV_HEADS, A_HEADS // A_KV_HEADS, A_HEAD_DIM
    nb = S // L
    qkv = h @ w_qkv + b_qkv
    q = qkv[..., :A_HEADS * hd].reshape(B, S, A_HEADS, hd)
    k = qkv[..., A_HEADS * hd:(A_HEADS + KV) * hd].reshape(B, S, KV, hd)
    v = qkv[..., (A_HEADS + KV) * hd:].reshape(B, S, KV, hd)
    q = partial_rope(q, pos, A_ROPE_DIM, ROPE_THETA)
    k = partial_rope(k, pos, A_ROPE_DIM, ROPE_THETA)
    qb = q.reshape(B, nb, L, KV, G, hd)
    kb = k.reshape(B, nb, L, KV, hd)
    vb = v.reshape(B, nb, L, KV, hd)
    kw = jnp.concatenate([jnp.concatenate([jnp.zeros_like(kb[:, :1]), kb[:, :-1]], axis=1), kb], axis=2)
    vw = jnp.concatenate([jnp.concatenate([jnp.zeros_like(vb[:, :1]), vb[:, :-1]], axis=1), vb], axis=2)
    scores = jnp.einsum('bnqkgd,bnskd->bnkgqs', qb, kw).astype(jnp.float32) * (hd ** -0.5)
    qi = jnp.arange(L)[:, None]
    kj = jnp.arange(2 * L)[None, :]
    rel = qi + L - kj
    band = (rel >= 0) & (rel < A_WINDOW)
    blk = jnp.arange(nb)[:, None, None]
    valid = band[None] & (blk * L + kj[None] - L >= 0)
    scores = jnp.where(valid[None, :, None, None], scores, -jnp.inf)
    sink = sinks.astype(jnp.float32).reshape(KV, G)[None, None, :, :, None, None]
    mx = jnp.maximum(jnp.max(scores, axis=-1, keepdims=True), sink)
    p = jnp.exp(scores - mx)
    probs = (p / (jnp.sum(p, axis=-1, keepdims=True) + jnp.exp(sink - mx))).astype(vw.dtype)
    o = jnp.einsum('bnkgqs,bnskd->bnqkgd', probs, vw).reshape(B, S, A_HEADS * hd)
    return o @ w_o + b_o

def mlstm_mixer(h, w_in, b_if, norm_w, w_out):
    B, S, _ = h.shape
    H, dk, dv, L = M_HEADS, M_QK_DIM, M_V_DIM, M_CHUNK
    N = S // L
    proj = h @ w_in
    c0, c1, c2, c3 = H * dk, 2 * H * dk, 2 * H * dk + H * dv, 2 * H * dk + 2 * H * dv
    q, k, v, o, gates = proj[..., :c0], proj[..., c0:c1], proj[..., c1:c2], proj[..., c2:c3], proj[..., c3:]
    gates = gates.astype(jnp.float32) + b_if.astype(jnp.float32)
    gates = M_GATE_CAP * jnp.tanh(gates / M_GATE_CAP)
    log_i = gates[..., :H]
    log_f = jax.nn.log_sigmoid(gates[..., H:])

    def chunks(t, d):
        return t.astype(jnp.float32).reshape(B, N, L, H, d).transpose(1, 0, 3, 2, 4)

    def gchunks(t):
        return t.reshape(B, N, L, H).transpose(1, 0, 3, 2)

    xs = (chunks(q, dk) * (dk ** -0.5), chunks(k, dk), chunks(v, dv), gchunks(log_i), gchunks(log_f))
    causal = jnp.tril(jnp.ones((L, L), dtype=bool))

    def step(carry, inp):
        C, n, m = carry
        qc, kc, vc, li, lf = inp
        b = jnp.cumsum(lf, axis=-1)
        dmat = jnp.where(causal, b[..., :, None] - b[..., None, :] + li[..., None, :], -jnp.inf)
        inter = b + m[..., None]
        m_row = jnp.maximum(inter, jnp.max(dmat, axis=-1))
        w_intra = jnp.exp(dmat - m_row[..., None])
        w_inter = jnp.exp(inter - m_row)
        s = jnp.einsum('bhtd,bhsd->bhts', qc, kc) * w_intra
        num = jnp.einsum('bhts,bhsv->bhtv', s, vc) + w_inter[..., None] * jnp.einsum('bhvd,bhtd->bhtv', C, qc)
        nq = jnp.sum(s, axis=-1) + w_inter * jnp.einsum('bhd,bhtd->bht', n, qc)
        h_out = num / jnp.maximum(jnp.abs(nq), jnp.exp(-m_row))[..., None]
        b_last = b[..., -1]
        dec = b_last[..., None] - b + li
        m_new = jnp.maximum(b_last + m, jnp.max(dec, axis=-1))
        wk = jnp.exp(dec - m_new[..., None])
        keep = jnp.exp(b_last + m - m_new)
        C_new = keep[..., None, None] * C + jnp.einsum('bhsv,bhsd->bhvd', vc * wk[..., None], kc)
        n_new = keep[..., None] * n + jnp.einsum('bhs,bhsd->bhd', wk, kc)
        return (C_new, n_new, m_new), h_out

    init = (jnp.zeros((B, H, dv, dk), jnp.float32), jnp.zeros((B, H, dk), jnp.float32), jnp.zeros((B, H), jnp.float32))
    _, hs = lax.scan(step, init, xs)
    hs = hs.transpose(1, 0, 3, 2, 4).reshape(B, S, H, dv)
    hs = hs * lax.rsqrt(jnp.mean(hs * hs, axis=-1, keepdims=True) + EPS)
    hs = hs.reshape(B, S, H * dv) * norm_w.astype(jnp.float32)
    return (jax.nn.sigmoid(o.astype(jnp.float32)) * hs).astype(h.dtype) @ w_out

def retention_mixer(h, pos, w_in, norm_w, w_out):
    B, S, _ = h.shape
    H, dk, dv, L = R_HEADS, R_QK_DIM, R_V_DIM, R_CHUNK
    N = S // L
    proj = h @ w_in
    c0, c1, c2 = H * dk, 2 * H * dk, 2 * H * dk + H * dv
    q = retnet_rotate(proj[..., :c0].reshape(B, S, H, dk), pos, R_THETA)
    k = retnet_rotate(proj[..., c0:c1].reshape(B, S, H, dk), pos, R_THETA) * (dk ** -0.5)
    v = proj[..., c1:c2].reshape(B, S, H, dv)
    g = proj[..., c2:]
    log_gamma = jnp.log(1.0 - 2.0 ** (-5.0 - jnp.arange(H, dtype=jnp.float32)))
    j = jnp.arange(L, dtype=jnp.float32)
    diff = j[:, None] - j[None, :]
    causal = diff >= 0
    dmask = jnp.where(causal, jnp.exp(jnp.where(causal, diff, 0.0) * log_gamma[:, None, None]), 0.0)
    q_decay = jnp.exp((j + 1.0) * log_gamma[:, None])
    k_decay = jnp.exp((L - 1.0 - j) * log_gamma[:, None])
    chunk_decay = jnp.exp(L * log_gamma)

    def chunks(t, d):
        return t.astype(jnp.float32).reshape(B, N, L, H, d).transpose(1, 0, 3, 2, 4)

    def step(state, inp):
        qc, kc, vc = inp
        inner = jnp.einsum('bhts,bhsv->bhtv', jnp.einsum('bhtd,bhsd->bhts', qc, kc) * dmask, vc)
        cross = jnp.einsum('bhtd,bhdv->bhtv', qc * q_decay[..., None], state)
        new_state = chunk_decay[:, None, None] * state + jnp.einsum('bhsd,bhsv->bhdv', kc * k_decay[..., None], vc)
        return new_state, inner + cross

    _, ys = lax.scan(step, jnp.zeros((B, H, dk, dv), jnp.float32), (chunks(q, dk), chunks(k, dk), chunks(v, dv)))
    y = ys.transpose(1, 0, 3, 2, 4).reshape(B, S, H, dv)
    mu = jnp.mean(y, axis=-1, keepdims=True)
    yc = y - mu
    y = yc * lax.rsqrt(jnp.mean(yc * yc, axis=-1, keepdims=True) + EPS)
    y = y.reshape(B, S, H * dv) * norm_w.astype(jnp.float32)
    return (jax.nn.silu(g.astype(jnp.float32)) * y).astype(h.dtype) @ w_out

def setup_inputs(seed: int = 0) -> dict:
    key = jax.random.key(seed)
    ks = jax.random.split(key, 20)
    f32 = jnp.float32

    def dense(k, shape, fan_in):
        return jax.random.normal(k, shape, f32) * (fan_in ** -0.5)

    x = jax.random.normal(ks[0], (BATCH, SEQ, D_MODEL), f32)
    offset = jax.random.randint(ks[1], (BATCH, 1), 0, 1024, dtype=jnp.int32)
    positions = offset + jnp.arange(SEQ, dtype=jnp.int32)[None, :]
    norm_w = 1.0 + 0.05 * jax.random.normal(ks[2], (DEPTH, 3, D_MODEL), f32)
    final_norm_w = 1.0 + 0.05 * jax.random.normal(ks[3], (D_MODEL,), f32)
    ffn_w_in = dense(ks[4], (DEPTH, 2, D_MODEL, 2 * D_FF), D_MODEL)
    ffn_w_out = dense(ks[5], (DEPTH, 2, D_FF, D_MODEL), D_FF)
    attn_w_qkv = dense(ks[6], (N_ATTN, D_MODEL, A_QKV_DIM), D_MODEL)
    attn_b_qkv = 0.02 * jax.random.normal(ks[7], (N_ATTN, A_QKV_DIM), f32)
    attn_w_o = dense(ks[8], (N_ATTN, A_HEADS * A_HEAD_DIM, D_MODEL), A_HEADS * A_HEAD_DIM)
    attn_b_o = 0.02 * jax.random.normal(ks[9], (N_ATTN, D_MODEL), f32)
    attn_sinks = 0.5 * jax.random.normal(ks[10], (N_ATTN, A_HEADS), f32)
    mlstm_w_in = dense(ks[11], (N_MLSTM, D_MODEL, M_IN_DIM), D_MODEL)
    f_bias = jnp.linspace(3.0, 6.0, M_HEADS, dtype=f32)[None, :]
    mlstm_b_if = jnp.concatenate([0.1 * jax.random.normal(ks[12], (N_MLSTM, M_HEADS), f32),
                                  f_bias + 0.1 * jax.random.normal(ks[13], (N_MLSTM, M_HEADS), f32)], axis=-1)
    mlstm_norm_w = 1.0 + 0.05 * jax.random.normal(ks[14], (N_MLSTM, M_HEADS * M_V_DIM), f32)
    mlstm_w_out = dense(ks[15], (N_MLSTM, M_HEADS * M_V_DIM, D_MODEL), M_HEADS * M_V_DIM)
    ret_w_in = dense(ks[16], (N_RET, D_MODEL, R_IN_DIM), D_MODEL)
    ret_norm_w = 1.0 + 0.05 * jax.random.normal(ks[17], (N_RET, R_HEADS * R_V_DIM), f32)
    ret_w_out = dense(ks[18], (N_RET, R_HEADS * R_V_DIM, D_MODEL), R_HEADS * R_V_DIM)
    return {'x': x, 'positions': positions, 'norm_w': norm_w, 'final_norm_w': final_norm_w,
            'ffn_w_in': ffn_w_in, 'ffn_w_out': ffn_w_out,
            'attn_w_qkv': attn_w_qkv, 'attn_b_qkv': attn_b_qkv, 'attn_w_o': attn_w_o, 'attn_b_o': attn_b_o,
            'attn_sinks': attn_sinks,
            'mlstm_w_in': mlstm_w_in, 'mlstm_b_if': mlstm_b_if, 'mlstm_norm_w': mlstm_norm_w, 'mlstm_w_out': mlstm_w_out,
            'ret_w_in': ret_w_in, 'ret_norm_w': ret_norm_w, 'ret_w_out': ret_w_out}

def reference(x, positions, norm_w, final_norm_w, ffn_w_in, ffn_w_out,
              attn_w_qkv, attn_b_qkv, attn_w_o, attn_b_o, attn_sinks,
              mlstm_w_in, mlstm_b_if, mlstm_norm_w, mlstm_w_out,
              ret_w_in, ret_norm_w, ret_w_out):
    for i in range(DEPTH):
        kind, slot = i % N_MIXERS, i // N_MIXERS
        x = x + 0.5 * swiglu(rms_norm(x, norm_w[i, 0]), ffn_w_in[i, 0], ffn_w_out[i, 0])
        hn = rms_norm(x, norm_w[i, 1])
        if kind == 0:
            mix = swa_sink_attention(hn, positions, attn_w_qkv[slot], attn_b_qkv[slot], attn_w_o[slot],
                                     attn_b_o[slot], attn_sinks[slot])
        elif kind == 1:
            mix = mlstm_mixer(hn, mlstm_w_in[slot], mlstm_b_if[slot], mlstm_norm_w[slot], mlstm_w_out[slot])
        else:
            mix = retention_mixer(hn, positions, ret_w_in[slot], ret_norm_w[slot], ret_w_out[slot])
        x = x + mix
        x = x + 0.5 * swiglu(rms_norm(x, norm_w[i, 2]), ffn_w_in[i, 1], ffn_w_out[i, 1])
    return rms_norm(x, final_norm_w)


_drawn_inputs = setup_inputs


def setup_inputs(seed=0):
    import zlib

    import numpy as np

    out = dict(_drawn_inputs(seed))
    spreads = {}
    factors = {}
    for name, (base, spread) in spreads.items():
        noise = np.random.default_rng([zlib.crc32(name.encode()), seed]).standard_normal(out[name].shape)
        drawn = base * np.exp(spread * noise) if base else spread * noise
        out[name] = jnp.asarray(drawn.astype(out[name].dtype))
    for name, factor in factors.items():
        out[name] = (out[name] * factor).astype(out[name].dtype)
    return out
```

```python
from contextlib import ExitStack

import numpy as np

import concourse.bass as bass
from concourse import mybir

F32 = mybir.dt.float32
F32R = mybir.dt.float32r
I32 = mybir.dt.int32
ALU = mybir.AluOpType
ACT = mybir.ActivationFunctionType
AX = mybir.AxisListType.X

P = 128
D = 1024
SEQ = 256
TT = SEQ // P
KD = D // P
FF = 2816
CH = 256
NCH = FF // CH
NB = 512
EPS = 1e-6
RING = 6
U = 1024
NEG = -1e30

HEADS, KVH, HD = 16, 4, 64
GRP = HEADS // KVH
ROPE_HALF = HD // 8
MH, MDK, MDV = 8, 64, 128
CAP = 15.0
RH, RDK, RDV = 4, 256, 512
TRI = 3 * P

PHASES = ["ffn", "attn", "ffn", "ffn", "mlstm", "ffn", "ffn", "ret", "ffn", "ffn", "attn", "ffn"]
PROJ = {"ffn": NCH, "attn": 3, "mlstm": 6, "ret": 12}
KOUT = {"ffn": 2 * NCH, "attn": 8, "mlstm": 8, "ret": 16}
TURNS = {"ffn": NCH, "attn": 4, "mlstm": 4, "ret": 8}

C_ID = 0
C_MA = C_ID + P
C_MB = C_MA + TRI
C_DM = C_MB + TRI
C_SEL = C_DM + RH * TRI
C_INV = C_SEL + MH * P
N_INV = ROPE_HALF + RDK // 2
C_ONE = C_INV + N_INV
N_CONST = C_ONE + SEQ


class Phase:

    def __init__(self, n, kind, unit, group, turn, ffn, mixer):
        self.n, self.kind, self.unit, self.group, self.turn = n, kind, unit, group, turn
        self.ffn, self.mixer = ffn, mixer


def plan():
    out, unit, group, turn, seen = [], 0, 0, 0, {}
    for n, kind in enumerate(PHASES):
        i = seen.get(kind, 0)
        seen[kind] = i + 1
        out.append(Phase(n, kind, unit, group, turn, i, i))
        unit += 4 * PROJ[kind] + KOUT[kind]
        group += TT * PROJ[kind]
        turn += 2 * TT + TURNS[kind]
    return out, unit


def constants():
    c = np.zeros((P, N_CONST), np.float32)
    c[:, C_ID:C_ID + P] = np.eye(P)
    i = np.arange(P)
    row, col = i[:, None], i[None, :]
    c[:, C_MA:C_MA + P] = np.where(col <= row, 0, NEG)
    c[:, C_MA + P:C_MA + 2 * P] = np.where(col > row, 0, NEG)
    c[:, C_MA + 2 * P:C_MA + 3 * P] = np.where(col <= row, 0, NEG)
    c[:, C_MB:C_MB + P] = np.where(col >= row, 0, NEG)
    c[:, C_MB + 2 * P:C_MB + 3 * P] = np.where(col >= row, 0, NEG)
    for h in range(RH):
        log_gamma = np.log1p(-2.0 ** (-5.0 - h))
        for b, away in ((0, 0), (1, P), (2, 0)):
            diff = col + away - row
            at = C_DM + h * TRI + b * P
            c[:, at:at + P] = np.where(diff >= 0, np.exp(np.maximum(diff, 0) * log_gamma), 0) * RDK ** -0.5
    for h in range(MH):
        c[h, C_SEL + h * P:C_SEL + (h + 1) * P] = 1
    rope = 1.0 / 500000.0 ** (np.arange(0, 2 * ROPE_HALF, 2) / (2.0 * ROPE_HALF))
    ret = 1.0 / 10000.0 ** np.linspace(0.0, 1.0, RDK // 2)
    c[:, C_INV:C_INV + N_INV] = np.concatenate([rope, ret])
    c[:, C_ONE:] = 1
    return c


def build(nc, x, positions, norm_w, final_norm_w, ffn_w_in, ffn_w_out, attn_w_qkv, attn_b_qkv, attn_w_o,
          attn_b_o, attn_sinks, mlstm_w_in, mlstm_b_if, mlstm_norm_w, mlstm_w_out, ret_w_in, ret_norm_w,
          ret_w_out, consts, out):
    phases, n_units = plan()
    ctx = ExitStack()
    with ctx:
        def sb(name, shape, dt=F32):
            return ctx.enter_context(nc.sbuf_tensor(name, shape, dt))

        def sem(name):
            return ctx.enter_context(nc.semaphore(name))

        const = sb("const", [P, N_CONST])
        ident = const[:, C_ID:C_ID + P]
        xs = sb("xs", [P, TT, D])
        xT_hi = sb("xT_hi", [P, KD, SEQ], F32R)
        xT_lo = sb("xT_lo", [P, KD, SEQ], F32R)
        zT_hi = sb("zT_hi", [P, KD, SEQ], F32R)
        zT_lo = sb("zT_lo", [P, KD, SEQ], F32R)
        raw = sb("raw", [P, RING, U])
        w_hi = sb("w_hi", [P, RING, U], F32R)
        w_lo = sb("w_lo", [P, RING, U], F32R)
        nw_rows = sb("nw_rows", [P, P])
        nw = sb("nw", [P, P])
        pos_i = sb("pos_i", [P, TT], I32)
        pos_f = sb("pos_f", [P, TT])
        cos = sb("cos", [P, TT, N_INV])
        sin = sb("sin", [P, TT, N_INV])
        sinks = sb("sinks", [P, 2, HEADS])
        wgate = sb("wgate", [P, KD, 2 * MH])
        bgate = sb("bgate", [P, 2 * MH])
        ssq = sb("ssq", [P, TT])
        rms = sb("rms", [P, TT])
        rstd = sb("rstd", [P, TT])
        eps = sb("eps", [P, 1])
        ARENA = 17300
        arena = sb("arena", [P, ARENA])

        acc = ctx.enter_context(nc.psum_tensor("acc", [P, 4, NB], F32))
        proj = ctx.enter_context(nc.psum_tensor("proj", [P, TT, NB], F32))
        turn = ctx.enter_context(nc.psum_tensor("turn", [P, 2, NB], F32))

        def carve(*shapes):
            at, views = 0, []
            for shape in shapes:
                n = int(np.prod(shape))
                v = arena[:, at:at + n]
                if len(shape) == 2:
                    v = v.rearrange("p (a b) -> p a b", a=shape[0])
                if len(shape) == 3:
                    v = v.rearrange("p (a b c) -> p a b c", a=shape[0], b=shape[1])
                views.append(v)
                at += n
            assert at <= ARENA, at
            return views

        f_gate, f_hid = carve((TT, CH), (TT, CH))
        _, t_ang, t_k, t_r, t_p, final_w = carve((2 * TT * CH,), *[(TT, N_INV)] * 4, (D,))
        (a_qkv, a_bias, a_bo, a_kdup, a_qT, a_kT, a_s0, a_s1, a_pT0, a_pT1, a_rot, a_mx, a_m, a_nm, a_se, a_sum,
         a_den, a_rden) = carve((TT, 1536), (1536,), (D,), (TT, 2 * KVH * HD), (8, SEQ), (KVH, SEQ), (GRP, TRI),
                                (GRP, TRI), (3, NB), (3, NB), (4, TT * 8 * ROPE_HALF), (4, 8), (4, 8), (4, 8),
                                (4, 8), (4, 8), (4, 8), (4, 8))
        a_s, a_pT = [a_s0, a_s1], [a_pT0, a_pT1]
        (m_qk, m_v, m_o, m_qT, m_kT, m_w0, m_w1, m_p0, m_p1, m_num, m_g, m_th, m_e, m_nl, m_C, m_a, m_M, m_cm,
         m_acol, m_em, m_ss, m_den, m_rd, m_t, m_rs, m_fs) = carve(
            (TT, 1024), (TT * MH, MDV + 1), (TT, 1024), (4, SEQ), (4, SEQ), (TRI,), (TRI,), (TRI,), (TRI,),
            (MH * TT, MDV + 1), (TT, 2 * MH), (TT, 2 * MH), (TT, MH), (TT, MH), (SEQ,), (SEQ,), (SEQ,), (SEQ,),
            (TT, MH), (TT, MH), (TT, MH), (TT, MH), (TT, MH), (TT, MH), (TT, MH), (TT, MH))
        m_w, m_p = [m_w0, m_w1], [m_p0, m_p1]
        (r_all, r_tmp, r_qk0, r_qk1, r_p0, r_p1, r_y0, r_y1, r_bn, r_mv, r_sd, r_rs) = carve(
            (TT, 6144), (4, 256), (2, 2 * SEQ), (2, 2 * SEQ), (TRI,), (TRI,), (NB,), (NB,), (RH * TT, 6),
            (RH * TT, 2), (RH * TT, 1), (RH * TT, 1))
        r_qk, r_p, r_y = [r_qk0, r_qk1], [r_p0, r_p1], [r_y0, r_y1]

        raw_in = [sem(f"raw_in{i}") for i in range(RING)]
        hi_done = sem("hi_done")
        split_done = sem("split_done")
        unit_used = sem("unit_used")
        proj_full = sem("proj_full")
        gate_done = sem("gate_done")
        proj_free = sem("proj_free")
        turn_full = sem("turn_full")
        turn_hi = sem("turn_hi")
        turn_free = sem("turn_free")
        acc_full = sem("acc_full")
        x_ready = sem("x_ready")
        x_in = [sem(f"x_in{t}") for t in range(TT)]
        ssq_done = sem("ssq_done")
        rms_done = sem("rms_done")
        rstd_ready = sem("rstd_ready")
        const_in = sem("const_in")
        tables_in = sem("tables_in")
        rows_in = sem("rows_in")
        nw_turned = sem("nw_turned")
        nw_ready = sem("nw_ready")
        eps_set = sem("eps_set")
        angles_ready = sem("angles_ready")
        sincos = sem("sincos")
        dve = sem("dve")
        pool = sem("pool")
        bias_in = sem("bias_in")
        bo_added = sem("bo_added")
        roped = sem("roped")
        a_turned = sem("a_turned")
        a_evac_a = sem("a_evac_a")
        a_evac_v = sem("a_evac_v")
        a_sfull = sem("a_sfull")
        a_masked = sem("a_masked")
        a_max = sem("a_max")
        a_exp = sem("a_exp")
        a_pfull = sem("a_pfull")
        a_pcopy_a = sem("a_pcopy_a")
        a_pcopy_v = sem("a_pcopy_v")
        a_ofull = sem("a_ofull")
        a_odone = sem("a_odone")
        m_ones = sem("m_ones")
        m_gfull = sem("m_gfull")
        m_graw = sem("m_graw")
        m_act = sem("m_act")
        m_rfull = sem("m_rfull")
        m_rows = sem("m_rows")
        m_cfull = sem("m_cfull")
        m_cols = sem("m_cols")
        m_emd = sem("m_emd")
        m_turned = sem("m_turned")
        m_tcopy = sem("m_tcopy")
        m_sfull = sem("m_sfull")
        m_wpre = sem("m_wpre")
        m_wexp = sem("m_wexp")
        m_pdone = sem("m_pdone")
        m_yfull = sem("m_yfull")
        m_ssd = sem("m_ssd")
        m_ycopy = sem("m_ycopy")
        m_var = sem("m_var")
        m_root = sem("m_root")
        m_sig = sem("m_sig")
        m_y = sem("m_y")
        r_rot = sem("r_rot")
        r_silu = sem("r_silu")
        r_turned = sem("r_turned")
        r_tcopy = sem("r_tcopy")
        r_sfull = sem("r_sfull")
        r_pdone = sem("r_pdone")
        r_yfull = sem("r_yfull")
        r_mvd = sem("r_mvd")
        r_sdd = sem("r_sdd")
        r_norm = sem("r_norm")
        r_gated = sem("r_gated")
        final_in = sem("final_in")
        out_done = sem("out_done")

        def slot(n):
            return n % RING

        def unit_threshold(n, c):
            return 16 * (n // RING + 1) + (c * 16 if not isinstance(c, int) else 16 * c)

        def count(base, c, step):
            return base + step * c if isinstance(c, int) else c * step + base

        def later(value, c, step):
            return value + step * (c if isinstance(c, int) else 2) > 0

        def split_hi(act, n, c=0):
            act.wait_ge(raw_in[slot(n)], unit_threshold(n, c))
            if later(n - RING + 1, c, RING):
                act.wait_ge(unit_used, count(n - RING + 1, c, RING))
            act.activation(w_hi[:, slot(n), :], raw[:, slot(n), :], ACT.Copy).then_inc(hi_done, 1)

        def split_lo(v, n, c=0):
            v.wait_ge(hi_done, count(n + 1, c, RING))
            v.tensor_tensor(w_lo[:, slot(n), :], raw[:, slot(n), :], w_hi[:, slot(n), :].bitcast(F32),
                            ALU.subtract).then_inc(split_done, 1)

        def projected(eng, ph, c, t):
            if t == 0:
                eng.wait_ge(proj_full, count(ph.group // 2 + 1, c, 1))
            elif ph.kind == "ffn" and not (isinstance(c, int) and c == 0):
                eng.wait_ge(unit_used, count(ph.unit + 2, c, RING))
            else:
                eng.wait_ge(unit_used, ph.unit + 4 * (c + 1))

        def accumulated(eng, ph, t, half):
            if t == 0 or half == 0:
                eng.wait_ge(acc_full, 3 * ph.n + 2 * t + half + 1)
            else:
                eng.wait_ge(unit_used, ph.unit + 4 * PROJ[ph.kind] + KOUT[ph.kind])

        def x_wait(eng, p, t, half):
            if p == 0:
                eng.wait_ge(x_in[t], 16)
            else:
                eng.wait_ge(x_ready, 4 * (p - 1) + 2 * t + half + 1)

        def norm_col(ph):
            return ph.n * KD

        block = ctx.enter_context(nc.Block())

        @block.sync
        def _(sp):
            def load(n, c, dst, src):
                if later(n - RING + 1, c, RING):
                    sp.wait_ge(split_done, count(n - RING + 1, c, RING))
                sp.dma_start(dst, src).then_inc(raw_in[slot(n)], 16)

            def ffn_in(ph, n, c, chunk):
                w = ffn_w_in[ph.ffn // 2, ph.ffn % 2].rearrange("(k p) (g m) -> p k g m", p=P, g=2)
                for q in range(4):
                    load(n + q, c, raw[:, slot(n + q), :].rearrange("p (k m) -> p k m", k=4),
                         w[:, q // 2 * 4:q // 2 * 4 + 4, q % 2, bass.ds(chunk * CH, CH)])

            def ffn_out(ph, n, c, chunk):
                w = ffn_w_out[ph.ffn // 2, ph.ffn % 2].rearrange("(j k p) m -> p j k m", p=P, k=2)
                for k in range(2):
                    load(n + k, c, raw[:, slot(n + k), :], w[:, chunk, k, :])

            for t in range(TT):
                sp.dma_start(xs[:, t, :], x[0, t * P:(t + 1) * P, :]).then_inc(x_in[t], 16)
            for ph in phases:
                if ph.kind == "ffn":
                    ffn_in(ph, ph.unit, 0, 0)

                    def chunk(c):
                        ffn_in(ph, ph.unit - 2, c, c)
                        ffn_out(ph, ph.unit + 2, c, c - 1)

                    chunk(1)
                    with sp.Fori(2, NCH) as c:
                        chunk(c)
                    ffn_out(ph, ph.unit + 6 * NCH - 2, 0, NCH - 1)
                    continue
                w_in, w_out = {"attn": (attn_w_qkv, attn_w_o), "mlstm": (mlstm_w_in, mlstm_w_out),
                               "ret": (ret_w_in, ret_w_out)}[ph.kind]
                wi = w_in[ph.mixer].rearrange("(k p) m -> p k m", p=P)
                wo = w_out[ph.mixer].rearrange("(k p) m -> p k m", p=P)
                for ch in range(PROJ[ph.kind]):
                    for q in range(4):
                        n = ph.unit + 4 * ch + q
                        load(n, 0, raw[:, slot(n), :].rearrange("p (k m) -> p k m", k=2),
                             wi[:, 2 * q:2 * q + 2, ch * NB:(ch + 1) * NB])
                for k in range(KOUT[ph.kind]):
                    n = ph.unit + 4 * PROJ[ph.kind] + k
                    load(n, 0, raw[:, slot(n), :], wo[:, k, :])
            for t in range(TT):
                sp.wait_ge(x_ready, 4 * len(phases) + t + 1)
                sp.dma_start(out[0, t * P:(t + 1) * P, :], xs[:, t, :]).then_inc(out_done, 16)
            sp.wait_ge(out_done, 16 * TT)

        @block.gpsimd
        def _(g):
            chain = [0]

            def link(ins):
                chain[0] += 1
                ins.then_inc(pool, 1)
                g.wait_ge(pool, chain[0])

            g.memset(eps[:], EPS).then_inc(eps_set, 1)
            g.dma_start(ident, consts[:, C_ID:C_ID + P]).then_inc(const_in, 16)
            n_mix = KD * 3 * 4
            g.dma_start(nw_rows[0:n_mix, :], norm_w.rearrange("l w (k f) -> (l w k) f", f=P)).then_inc(rows_in, 16)
            g.dma_start(nw_rows[n_mix:n_mix + 8, :], mlstm_norm_w.rearrange("o (k f) -> (o k) f", f=P)) \
                .then_inc(rows_in, 16)
            g.dma_start(nw_rows[n_mix + 8:n_mix + 24, :], ret_norm_w.rearrange("o (k f) -> (o k) f", f=P)) \
                .then_inc(rows_in, 16)
            g.dma_start(const[:, P:N_CONST], consts[:, P:N_CONST]).then_inc(tables_in, 16)
            g.dma_start(pos_i[:, :], positions[0].rearrange("(t p) -> p t", p=P),
                        allow_slow_non_contiguous=True).then_inc(tables_in, 16)
            g.dma_start(sinks[:, :, :], attn_sinks.rearrange("(o s) h -> o s h", o=1).to_broadcast([P, 2, HEADS])) \
                .then_inc(tables_in, 16)
            g.dma_start(wgate[:, :, :], mlstm_w_in[0].rearrange("(k p) m -> p k m", p=P)[:, :, 3072:3088]) \
                .then_inc(tables_in, 16)
            g.dma_start(bgate[:, :], mlstm_b_if.to_broadcast([P, 2 * MH])).then_inc(tables_in, 16)

            def angles():
                two_pi = 2 * np.pi
                magic = 1.5 * 2.0 ** 23
                parts, rest = [], two_pi
                for scale in (2.0 ** 5, 2.0 ** 13, 2.0 ** 21):
                    part = np.floor(rest * scale) / scale
                    parts.append(part)
                    rest -= part
                parts.append(rest)
                g.wait_ge(tables_in, 16 * 5)
                link(g.tensor_copy(pos_f[:, :], pos_i[:, :]))
                for t in range(TT):
                    last = g.tensor_scalar(t_ang[:, t, :], const[:, C_INV:C_INV + N_INV], pos_f[:, t:t + 1], None,
                                           ALU.mult)
                link(last)
                limit = float(np.nextafter(np.float32(np.pi), np.float32(0)))
                for j, dst in enumerate((t_r, t_k)):
                    turns = cos
                    link(g.tensor_scalar(turns[:, :, :], t_ang, 1 / two_pi, 0.25 * j, ALU.mult, ALU.add))
                    link(g.tensor_scalar(turns[:, :, :], turns[:, :, :], magic, None, ALU.add))
                    link(g.tensor_scalar(turns[:, :, :], turns[:, :, :], magic, None, ALU.subtract))
                    src = t_ang
                    for part in parts:
                        link(g.tensor_scalar(t_p, turns[:, :, :], float(part), None, ALU.mult))
                        link(g.tensor_tensor(dst, src, t_p, ALU.subtract))
                        src = dst
                    if j:
                        link(g.tensor_scalar(dst, dst, float(np.pi / 2), None, ALU.add))
                    ins = g.tensor_scalar(dst, dst, limit, -limit, ALU.min, ALU.max)
                    link(ins) if not j else ins.then_inc(angles_ready, 1)

            angles()

            def attn(ph):
                i = ph.mixer
                g.wait_ge(x_ready, 4 * ph.n)
                g.wait_ge(sincos, 2)
                g.dma_start(a_bias, attn_b_qkv[i:i + 1, :].to_broadcast([P, 1536])).then_inc(bias_in, 16)
                g.dma_start(a_bo, attn_b_o[i:i + 1, :].to_broadcast([P, D])).then_inc(bias_in, 16)
                g.wait_ge(bias_in, 32 * (i + 1))
                for ch, nh in ((0, 8), (1, 8), (2, 4)):
                    g.wait_ge(proj_free, ph.group + 2 * ch + 2)
                    v = a_qkv[:, :, ch * NB:ch * NB + nh * HD].rearrange("p t (h e) -> p t h e", e=HD)
                    rot = [a_rot[:, j, 0:TT * nh * ROPE_HALF].rearrange("p (t h e) -> p t h e", t=TT, h=nh)
                           for j in range(4)]
                    for t in range(TT):
                        x1, x2 = v[:, t, :, 0:ROPE_HALF], v[:, t, :, ROPE_HALF:2 * ROPE_HALF]
                        co = cos[:, t:t + 1, 0:ROPE_HALF].to_broadcast([P, nh, ROPE_HALF])
                        si = sin[:, t:t + 1, 0:ROPE_HALF].to_broadcast([P, nh, ROPE_HALF])
                        g.tensor_tensor(rot[0][:, t], x1, co, ALU.mult)
                        g.tensor_tensor(rot[1][:, t], x2, si, ALU.mult)
                        g.tensor_tensor(rot[2][:, t], x2, co, ALU.mult)
                        link(g.tensor_tensor(rot[3][:, t], x1, si, ALU.mult))
                        g.tensor_tensor(x1, rot[0][:, t], rot[1][:, t], ALU.subtract)
                        last = g.tensor_tensor(x2, rot[2][:, t], rot[3][:, t], ALU.add)
                        if ch == 2:
                            link(last)
                            for j in range(2):
                                last = g.tensor_copy(
                                    a_kdup[:, t, :].rearrange("p (h j e) -> p h j e", h=KVH, j=2)[:, :, j, :],
                                    v[:, t, 0:KVH, :])
                    last.then_inc(roped, 1)
                for t in range(TT):
                    last = g.tensor_tensor(xs[:, t, :], xs[:, t, :], a_bo, ALU.add)
                last.then_inc(bo_added, 1)

            def mlstm(ph):
                g.wait_ge(x_ready, 4 * ph.n)
                g.memset(m_v[:, :, MDV:MDV + 1], 1.0).then_inc(m_ones, 1)

            def ret(ph):
                for h in range(RH):
                    for t in range(TT):
                        n = TT * h + t
                        g.wait_ge(r_norm, n + 1)
                        g.wait_ge(r_silu, 1)
                        y = r_all[:, t, 4096 + h * RDV:4096 + (h + 1) * RDV]
                        g.tensor_tensor(y, y, r_y[n % 2], ALU.mult).then_inc(r_gated, 1)

            for ph in phases:
                if ph.kind == "attn":
                    attn(ph)
                if ph.kind == "mlstm":
                    mlstm(ph)
                if ph.kind == "ret":
                    ret(ph)
            g.wait_ge(x_ready, 4 * (len(phases) - 1))
            g.dma_start(final_w, final_norm_w.rearrange("(o m) -> o m", o=1).to_broadcast([P, D])).then_inc(final_in, 16)

        @block.tensor
        def _(pe):
            def turn_x(p, t):
                for half in range(2):
                    x_wait(pe, p, t, half)
                    for k in range(4):
                        f = (4 * half + k) * P
                        last = pe.transpose(turn[:, half, k * P:(k + 1) * P], xs[:, t, f:f + P], ident)
                    last.then_inc(turn_full, 1)

            def three(dst, a, w, start, stop):
                pe.matmul(dst, a[0], w[0], start=start, stop=False)
                pe.matmul(dst, a[0], w[1], start=False, stop=False)
                return pe.matmul(dst, a[1], w[0], start=False, stop=stop)

            def project(ph, n, c, group, t, quarters=range(4)):
                gated = ph.kind == "ffn"
                for q in quarters:
                    if t == 0:
                        pe.wait_ge(split_done, count(n + q + (2 - q % 2 if gated else 1), c, RING))
                    if q == 0 and later(group - 1, c, TT):
                        pe.wait_ge(proj_free, count(group - 1, c, TT))
                    for k in (2 * q, 2 * q + 1):
                        if gated:
                            s = slot(n + q // 2 * 2)
                            w = [x_[:, s:s + 2, k % 4 * CH:(k % 4 + 1) * CH] for x_ in (w_hi, w_lo)]
                        else:
                            w = [x_[:, slot(n + q), k % 2 * NB:(k % 2 + 1) * NB] for x_ in (w_hi, w_lo)]
                        a = [x_[:, k, t * P:(t + 1) * P] for x_ in (xT_hi, xT_lo)]
                        last = three(proj[:, t, :], a, w, k == 0, k == KD - 1)
                    if t == 1 and (q % 2 or not gated):
                        last.then_inc(unit_used, 2 if gated else 1)
                if q == 3 and t == 0:
                    last.then_inc(proj_full, 1)

            def first_chunk(ph):
                pe.wait_ge(turn_free, ph.turn + 1)
                project(ph, ph.unit, 0, ph.group, 0, range(0, 2))
                pe.wait_ge(turn_free, ph.turn + 2)
                turn_x(ph.n, 1)
                project(ph, ph.unit, 0, ph.group, 0, range(2, 4))
                pe.wait_ge(turn_free, ph.turn + 4)
                project(ph, ph.unit, 0, ph.group + 1, 1)

            def out_pair(n, c, z, first, last_pair, between=None, ends=None):
                for k in range(2):
                    pe.wait_ge(split_done, count(n + k + 1, c, RING))
                    if last_pair and k == 0:
                        continue
                    if last_pair:
                        break
                    for t in range(TT):
                        for h in range(2):
                            w = [x_[:, slot(n + k), h * NB:(h + 1) * NB] for x_ in (w_hi, w_lo)]
                            a = [x_[:, z[k][1], t * P:(t + 1) * P] for x_ in z[k][0]]
                            last = three(acc[:, 2 * t + h, :], a, w, first and k == 0, False)
                    last.then_inc(unit_used, 1)
                    if k == 0 and between:
                        between()
                if last_pair:
                    for t in range(TT):
                        for h in range(2):
                            if t == 1 and h == 1 and ends:
                                ends()
                            for k in range(2):
                                w = [x_[:, slot(n + k), h * NB:(h + 1) * NB] for x_ in (w_hi, w_lo)]
                                a = [x_[:, z[k][1], t * P:(t + 1) * P] for x_ in z[k][0]]
                                last = three(acc[:, 2 * t + h, :], a, w, False, k == 1)
                                if t == 1 and h == 1:
                                    last.then_inc(unit_used, 1)
                            if t == 0 or h == 0:
                                last.then_inc(acc_full, 1)

            def z_pair(k):
                return [((zT_hi, zT_lo), k), ((zT_hi, zT_lo), k + 1)]

            def next_turn(ph):
                if ph.n + 1 < len(phases):
                    turn_x(ph.n + 1, 0)

            def turn_hidden(ph, c, bank):
                pe.wait_ge(proj_free, count(ph.group + 2, c, TT))
                for k in range(2):
                    for t in range(TT):
                        last = pe.transpose(turn[:, bank, k * SEQ + t * P:k * SEQ + (t + 1) * P],
                                            f_hid[:, t, k * P:(k + 1) * P], ident)
                last.then_inc(turn_full, 1)

            def ffn(ph):
                first_chunk(ph)
                tu = ph.turn + 2 * TT

                def chunk(c, first=False, last=False):
                    n = ph.unit - 2
                    project(ph, n, c, ph.group, 0)
                    turn_hidden(ph, c - 1, 0)
                    project(ph, n, c, ph.group + 1, 1)
                    pe.wait_ge(turn_free, count(tu, c, 1))
                    out_pair(n + 4, c, z_pair(0), first, False,
                             (lambda: turn_hidden(ph, c, 1)) if last else None)

                chunk(1, first=True)
                with pe.Fori(2, NCH - 1) as c:
                    chunk(c)
                chunk(NCH - 1, last=True)
                pe.wait_ge(turn_free, tu + NCH)
                out_pair(ph.unit + 6 * NCH - 2, 0, z_pair(2), False, True, ends=lambda: next_turn(ph))

            def mixer_out(ph, pairs):
                n = ph.unit + 4 * PROJ[ph.kind]
                for i, z in enumerate(pairs):
                    last = i == len(pairs) - 1
                    pe.wait_ge(turn_free, ph.turn + 2 * TT + i + 1)
                    out_pair(n + 2 * i, 0, z, i == 0, last, ends=lambda: next_turn(ph))

            def attn(ph):
                i = ph.mixer
                first_chunk(ph)
                for ch in (1, 2):
                    for t in range(TT):
                        project(ph, ph.unit + 4 * ch, 0, ph.group + 2 * ch + t, t)
                for b in range(6):
                    pe.wait_ge(roped, 3 * i + (b // 2 + 1))
                    for j in range(2):
                        for t in range(TT):
                            f = (2 * b + j) * P if b < 4 else (2 * (b - 4) + j) * P
                            src = a_qkv if b < 4 else a_kdup
                            dst = acc[:, b, :] if b < 4 else turn[:, b - 4, :]
                            last = pe.transpose(dst[:, j * SEQ + t * P:j * SEQ + (t + 1) * P],
                                                src[:, t, f:f + P], ident)
                    last.then_inc(a_turned, 1)

                def scores(g):
                    if g == 0:
                        pe.wait_ge(a_evac_a, 3 * (i + 1))
                        pe.wait_ge(a_evac_v, 3 * (i + 1))
                    else:
                        pe.wait_ge(a_masked, 4 * i + g)
                    for h in range(GRP):
                        pair, at = (GRP * g + h) // 2, h % 2 * HD
                        for t in range(TT):
                            q = a_qT[at:at + HD, pair, t * P:(t + 1) * P]
                            last = pe.matmul(acc[:, h, t * P:t * P + (t + 1) * P], q,
                                             a_kT[at:at + HD, g, 0:(t + 1) * P], start=True, stop=True)
                    last.then_inc(a_sfull, 1)

                def values(g):
                    pe.wait_ge(a_exp, 4 * i + g + 1)
                    if g:
                        pe.wait_ge(a_pcopy_a, 2 * (4 * i + g))
                        pe.wait_ge(a_pcopy_v, 4 * i + g)
                    banks = [proj[:, 0, :], proj[:, 1, :], turn[:, 0, :]]
                    for b in range(3):
                        for h in range(GRP):
                            last = pe.transpose(banks[b][:, h * P:(h + 1) * P],
                                                a_s[g % 2][:, h, b * P:(b + 1) * P], ident)
                        last.then_inc(a_pfull, 1)
                    pe.wait_ge(a_pcopy_a, 2 * (4 * i + g + 1))
                    pe.wait_ge(a_pcopy_v, 4 * i + g + 1)
                    if g:
                        pe.wait_ge(a_odone, 4 * i + g)
                    for t in range(TT):
                        for h in range(GRP):
                            dst = turn[:, 1, (t * GRP + h) * HD:(t * GRP + h + 1) * HD]
                            for s in range(t + 1):
                                last = pe.matmul(dst, a_pT[g % 2][:, t + s, h * P:(h + 1) * P],
                                                 a_qkv[:, s, 1280 + g * HD:1280 + (g + 1) * HD],
                                                 start=(s == 0), stop=(s == t))
                    last.then_inc(a_ofull, 1)

                scores(0)
                for g in range(KVH):
                    if g + 1 < KVH:
                        scores(g + 1)
                    values(g)
                pe.wait_ge(a_odone, 4 * (i + 1))
                for b in range(4):
                    if b >= 2:
                        pe.wait_ge(turn_free, ph.turn + 2 * TT + b - 1)
                    for j in range(2):
                        for t in range(TT):
                            f = (2 * b + j) * P
                            last = pe.transpose(turn[:, b % 2, j * SEQ + t * P:j * SEQ + (t + 1) * P],
                                                a_qkv[:, t, f:f + P], ident)
                    last.then_inc(turn_full, 1)
                mixer_out(ph, [z_pair(2 * b) for b in range(4)])

            def mlstm(ph):
                first_chunk(ph)
                pe.wait_ge(tables_in, 16 * 5)
                for t in range(TT):
                    for k in range(KD):
                        for j, part in enumerate((xT_hi, xT_lo)):
                            last = pe.matmul(turn[:, 0, t * 2 * MH:(t + 1) * 2 * MH],
                                             part[:, k, t * P:(t + 1) * P].bitcast(F32), wgate[:, k, :],
                                             start=(k + j == 0), stop=(k == KD - 1 and j == 1))
                last.then_inc(m_gfull, 1)
                for ch in range(1, 6):
                    for t in range(TT):
                        project(ph, ph.unit + 4 * ch, 0, ph.group + 2 * ch + t, t)
                    if ch == 2:
                        pe.wait_ge(proj_free, ph.group + 4)
                        for b in range(4):
                            for j in range(2):
                                for t in range(TT):
                                    f = (2 * b + j) * P
                                    last = pe.transpose(acc[:, b, j * SEQ + t * P:j * SEQ + (t + 1) * P],
                                                        m_qk[:, t, f:f + P], ident)
                            last.then_inc(m_turned, 1)
                        pe.wait_ge(m_act, 3)
                        for j, src in enumerate((m_th, m_nl)):
                            for t in range(TT):
                                last = pe.transpose(turn[0:MH, 1, (2 * j + t) * P:(2 * j + t + 1) * P],
                                                    src[:, t, 0:MH], ident)
                        last.then_inc(m_rfull, 1)
                    if ch == 4:
                        pe.wait_ge(m_rows, 1)
                        for j, src in enumerate((m_a, m_cm)):
                            for t in range(TT):
                                last = pe.transpose(turn[:, 0, (2 * j + t) * MH:(2 * j + t + 1) * MH],
                                                    src[0:MH, t * P:(t + 1) * P], ident[0:MH, 0:MH])
                        last.then_inc(m_cfull, 1)

                def scores(h):
                    b, at, pair = h % 2, h % 2 * MDK, h // 2
                    if h == 0:
                        pe.wait_ge(m_tcopy, 4)
                    if h >= 2:
                        pe.wait_ge(m_pdone, h - 1)
                    for s in range(TT):
                        pe.matmul(acc[:, b, s * SEQ:s * SEQ + (TT - s) * P], m_kT[at:at + MDK, pair, s * P:(s + 1) * P],
                                  m_qT[at:at + MDK, pair, s * P:SEQ], start=True, stop=True)
                    for s in range(TT):
                        last = pe.matmul(acc[:, 2 + b, s * SEQ:s * SEQ + (TT - s) * P],
                                         const[0:MH, C_SEL + h * P:C_SEL + (h + 1) * P], m_M[0:MH, s * P:SEQ],
                                         start=True, stop=True)
                    last.then_inc(m_sfull, 1)

                def values(h):
                    pe.wait_ge(m_pdone, h + 1)
                    if h >= 2:
                        pe.wait_ge(m_ycopy, h - 1)
                    else:
                        pe.wait_ge(proj_free, ph.group + 12)
                    pe.wait_ge(m_ones, 1)
                    for t in range(TT):
                        for s in range(t + 1):
                            last = pe.matmul(proj[:, h % 2, t * (MDV + 1):(t + 1) * (MDV + 1)],
                                             m_p[h % 2][:, (t + s) * P:(t + s + 1) * P], m_v[:, s * MH + h, :],
                                             start=(s == 0), stop=(s == t))
                    last.then_inc(m_yfull, 1)

                scores(0)
                for h in range(MH):
                    if h + 1 < MH:
                        scores(h + 1)
                    values(h)
                for b in range(4):
                    pe.wait_ge(m_y, 2 * (b + 1))
                    if b >= 2:
                        pe.wait_ge(turn_free, ph.turn + 2 * TT + b - 1)
                    for j in range(2):
                        for t in range(TT):
                            f = (2 * b + j) * P
                            last = pe.transpose(turn[:, b % 2, j * SEQ + t * P:j * SEQ + (t + 1) * P],
                                                m_o[:, t, f:f + P], ident)
                    last.then_inc(turn_full, 1)
                mixer_out(ph, [z_pair(2 * b) for b in range(4)])

            def ret(ph):
                first_chunk(ph)
                for ch in range(1, 12):
                    for t in range(TT):
                        project(ph, ph.unit + 4 * ch, 0, ph.group + 2 * ch + t, t)

                def turned(h):
                    if h == 0:
                        pe.wait_ge(r_rot, TT * 4)
                    else:
                        pe.wait_ge(r_tcopy, 2 * h)
                    for j in range(2):
                        for half in range(2):
                            for t in range(TT):
                                f = j * D + h * RDK
                                src = r_all[:, t, f:f + RDK].rearrange("p (e two) -> p two e", two=2)[:, half, :]
                                last = pe.transpose(acc[:, j, half * SEQ + t * P:half * SEQ + (t + 1) * P], src, ident)
                        last.then_inc(r_turned, 1)

                def scores(h):
                    pe.wait_ge(r_tcopy, 2 * (h + 1))
                    if h:
                        pe.wait_ge(r_pdone, h)
                    qT, kT = r_qk[h % 2][:, 0, :], r_qk[h % 2][:, 1, :]
                    for s in range(TT):
                        for half in range(2):
                            at = half * SEQ
                            last = pe.matmul(acc[:, 2, s * SEQ:s * SEQ + (TT - s) * P],
                                             kT[:, at + s * P:at + (s + 1) * P], qT[:, at + s * P:at + SEQ],
                                             start=(half == 0), stop=(half == 1))
                    last.then_inc(r_sfull, 1)

                def values(h):
                    pe.wait_ge(r_pdone, h + 1)
                    for t in range(TT):
                        if h:
                            pe.wait_ge(r_norm, TT * (h - 1) + t + 1)
                        dst = acc[:, 3, :] if t == 0 else proj[:, 0, :]
                        for s in range(t + 1):
                            last = pe.matmul(dst, r_p[h % 2][:, (t + s) * P:(t + s + 1) * P],
                                             r_all[:, s, 2048 + h * RDV:2048 + (h + 1) * RDV],
                                             start=(s == 0), stop=(s == t))
                        last.then_inc(r_yfull, 1)

                def turn_y(h):
                    pe.wait_ge(r_gated, TT * (h + 1))
                    for b in range(2):
                        n = ph.turn + 2 * TT + 2 * h + b
                        if h:
                            pe.wait_ge(turn_free, n - 1)
                        for j in range(2):
                            for t in range(TT):
                                f = 4096 + h * RDV + (2 * b + j) * P
                                last = pe.transpose(turn[:, b, j * SEQ + t * P:j * SEQ + (t + 1) * P],
                                                    r_all[:, t, f:f + P], ident)
                        last.then_inc(turn_full, 1)

                pe.wait_ge(proj_free, ph.group + 24)
                for h in range(RH + 2):
                    if h < RH:
                        turned(h)
                        scores(h)
                    if 1 <= h <= RH:
                        values(h - 1)
                    if h >= 2:
                        turn_y(h - 2)
                mixer_out(ph, [[((xT_hi, xT_lo), 2 * b), ((xT_hi, xT_lo), 2 * b + 1)] for b in range(4)] +
                          [z_pair(2 * b) for b in range(4)])

            pe.wait_ge(const_in, 16)
            pe.wait_ge(rows_in, 48)
            pe.transpose(acc[:, 0, 0:120], nw_rows[0:120, :], ident[0:120, 0:120]).then_inc(nw_turned, 1)
            turn_x(0, 0)
            for ph in phases:
                {"ffn": ffn, "attn": attn, "mlstm": mlstm, "ret": ret}[ph.kind](ph)

        @block.scalar
        def _(act):
            def x_hi(ph, t):
                for half in range(2):
                    act.wait_ge(turn_full, ph.turn + 2 * t + half + 1)
                    for k in range(4):
                        f = 4 * half + k
                        last = act.activation(xT_hi[:, f, t * P:(t + 1) * P], turn[:, half, k * P:(k + 1) * P],
                                              ACT.Copy, scale=nw[:, norm_col(ph) + f:norm_col(ph) + f + 1])
                    last.then_inc(turn_hi, 1)

            def statistics(p, t):
                x_wait(act, p, t, 0)
                x_wait(act, p, t, 1)
                act.activation(acc[:, 2 * t:2 * t + 2, :].rearrange("p a b -> p (a b)"), xs[:, t, :], ACT.Square,
                               accum_out=ssq[:, t:t + 1]).then_inc(ssq_done, 1)
                act.wait_ge(ssq_done, TT * p + t + 1)
                act.activation(rms[:, t:t + 1], ssq[:, t:t + 1], ACT.Sqrt, scale=1.0 / D, bias=eps[:, 0:1]) \
                   .then_inc(rms_done, 1)

            def start(ph):
                x_hi(ph, 0)
                statistics(ph.n, 0)
                x_hi(ph, 1)
                statistics(ph.n, 1)

            def silu_gate(ph, c, t):
                projected(act, ph, c, t)
                act.activation(f_gate[:, t, :], proj[:, t, 0:CH], ACT.Silu, scale=rstd[:, t:t + 1]) \
                   .then_inc(gate_done, 1)

            def turned_hi(bank, k, threshold):
                act.wait_ge(turn_full, threshold)
                act.activation(zT_hi[:, k:k + 2, :].rearrange("p a b -> p (a b)"), turn[:, bank, :], ACT.Copy) \
                   .then_inc(turn_hi, 1)

            def ffn(ph, final):
                start(ph)
                act.wait_ge(rstd_ready, TT * ph.n + TT)
                silu_gate(ph, 0, 0)
                for q in range(3):
                    split_hi(act, ph.unit + 4 + q)
                silu_gate(ph, 0, 1)
                split_hi(act, ph.unit + 7)

                def chunk(c, ahead=4):
                    n = ph.unit + 2
                    split_hi(act, n, c)
                    split_hi(act, n + 1, c)
                    turned_hi(0, 0, count(ph.turn + 2 * TT, c, 1))
                    silu_gate(ph, c, 0)
                    for q in range(min(ahead, 3)):
                        split_hi(act, n + 2 + q, c)
                    silu_gate(ph, c, 1)
                    if ahead == 4:
                        split_hi(act, n + 5, c)

                chunk(1)
                with act.Fori(2, NCH - 1) as c:
                    chunk(c)
                if ph.n == 0:
                    act.wait_ge(angles_ready, 1)
                    for table, angle in ((sin, t_r), (cos, t_k)):
                        act.activation(table[:, :, :], angle, ACT.Sin).then_inc(sincos, 1)
                chunk(NCH - 1, 2 if final else 4)
                turned_hi(1, 2, ph.turn + 2 * TT + NCH)
                if not final:
                    split_hi(act, ph.unit + 6 * NCH + 2)
                    split_hi(act, ph.unit + 6 * NCH + 3)

            def mixer_in(ph, n_chunks, extra):
                for ch in range(n_chunks):
                    for q in range(4):
                        split_hi(act, ph.unit + 4 * (ch + 1) + q)
                    if ch in extra:
                        extra[ch]()
                for q in range(2):
                    split_hi(act, ph.unit + 4 * (n_chunks + 1) + q)

            def mixer_out(ph):
                for i in range(KOUT[ph.kind] - 2):
                    split_hi(act, ph.unit + 4 * (PROJ[ph.kind] + 1) + 2 + i)

            def attn(ph):
                i = ph.mixer
                start(ph)
                mixer_in(ph, 3, {})
                for b in (0, 2, 4):
                    act.wait_ge(a_turned, 6 * i + b + 1)
                    dst = a_qT[:, 2 * b:2 * b + 2, :] if b < 4 else a_kT[:, 0:2, :]
                    src = acc[:, b, :] if b < 4 else turn[:, 0, :]
                    act.activation(dst.rearrange("p a b -> p (a b)"), src, ACT.Copy).then_inc(a_evac_a, 1)

                def probabilities(g):
                    act.wait_ge(a_max, 4 * i + g + 1)
                    act.activation(a_se[:, g, :], a_se[:, g, :], ACT.Exp)
                    for t in range(TT):
                        for h in range(GRP):
                            s = a_s[g % 2][:, h, t * P:t * P + (t + 1) * P]
                            j = t * GRP + h
                            last = act.activation(s, s, ACT.Exp, scale=HD ** -0.5, bias=a_nm[:, g, j:j + 1],
                                                  accum_out=a_sum[:, g, j:j + 1])
                    last.then_inc(a_exp, 1)

                def copies(g):
                    for b in range(2):
                        act.wait_ge(a_pfull, 3 * (4 * i + g) + b + 1)
                        act.activation(a_pT[g % 2][:, b, :], proj[:, b, :], ACT.Copy).then_inc(a_pcopy_a, 1)

                probabilities(0)
                for g in range(KVH):
                    if g + 1 < KVH:
                        probabilities(g + 1)
                    copies(g)
                for b in range(4):
                    turned_hi(b % 2, 2 * b, ph.turn + 2 * TT + b + 1)
                mixer_out(ph)

            def mlstm(ph):
                start(ph)

                def gates():
                    act.wait_ge(m_graw, 1)
                    act.activation(m_th[:, :, :], m_g[:, :, :], ACT.Tanh, scale=1 / CAP).then_inc(m_act, 1)
                    act.wait_ge(m_act, 1)
                    act.activation(m_e[:, :, :], m_th[:, :, MH:2 * MH], ACT.Exp, scale=-CAP).then_inc(m_act, 1)
                    act.wait_ge(m_act, 2)
                    act.activation(m_nl[:, :, :], m_e[:, :, :], ACT.Ln, bias=1.0).then_inc(m_act, 1)

                def turned_qk():
                    for b in range(4):
                        act.wait_ge(m_turned, b + 1)
                        dst = m_qT[:, 2 * b:2 * b + 2, :] if b < 2 else m_kT[:, 2 * b - 4:2 * b - 2, :]
                        act.activation(dst.rearrange("p a b -> p (a b)"), acc[:, b, :], ACT.Copy,
                                       scale=MDK ** -0.5 if b < 2 else 1.0).then_inc(m_tcopy, 1)

                mixer_in(ph, 6, {0: gates, 2: turned_qk})
                act.wait_ge(m_cfull, 1)
                act.activation(m_em[:, :, :].rearrange("p a b -> p (a b)"), turn[:, 0, 2 * MH:4 * MH], ACT.Exp) \
                   .then_inc(m_emd, 1)
                act.wait_ge(m_cols, 1)

                def weights(h):
                    act.wait_ge(m_wpre, h + 1)
                    w = m_w[h % 2]
                    act.activation(w[:, 0:SEQ], w[:, 0:SEQ], ACT.Exp, bias=m_acol[:, 0, h:h + 1])
                    act.activation(w[:, SEQ:TRI], w[:, SEQ:TRI], ACT.Exp, bias=m_acol[:, 1, h:h + 1]) \
                       .then_inc(m_wexp, 1)

                def squares(h):
                    act.wait_ge(m_yfull, h + 1)
                    if h:
                        act.wait_ge(m_ssd, h)
                    for t in range(TT):
                        y = proj[:, h % 2, t * (MDV + 1):t * (MDV + 1) + MDV]
                        last = act.activation(turn[:, 0, 128 + t * P:128 + (t + 1) * P], y, ACT.Square,
                                              accum_out=m_ss[:, t, h:h + 1])
                    last.then_inc(m_ssd, 1)

                weights(0)
                for h in range(MH):
                    if h + 1 < MH:
                        weights(h + 1)
                    squares(h)
                act.wait_ge(proj_free, ph.group + 12)
                act.activation(m_o[:, :, :], m_o[:, :, :], ACT.Sigmoid).then_inc(m_sig, 1)
                act.wait_ge(m_var, 1)
                act.activation(m_rs[:, :, :], m_t[:, :, :], ACT.Sqrt, scale=1 / MDV, bias=eps[:, 0:1]) \
                   .then_inc(m_root, 1)
                for b in range(4):
                    act.wait_ge(turn_full, ph.turn + 2 * TT + b + 1)
                    for j in range(2):
                        k = 2 * b + j
                        last = act.activation(zT_hi[:, k, :], turn[:, b % 2, j * SEQ:(j + 1) * SEQ], ACT.Copy,
                                              scale=nw[:, 96 + k:97 + k])
                    last.then_inc(turn_hi, 1)
                mixer_out(ph)

            def ret(ph):
                start(ph)
                mixer_in(ph, 12, {})
                act.wait_ge(proj_free, ph.group + 24)
                act.activation(r_all[:, :, 4096:6144], r_all[:, :, 4096:6144], ACT.Silu).then_inc(r_silu, 1)

                def turned(h):
                    for j in range(2):
                        act.wait_ge(r_turned, 2 * h + j + 1)
                        act.activation(r_qk[h % 2][:, j, :], acc[:, j, :], ACT.Copy).then_inc(r_tcopy, 1)

                def deviations(h):
                    for t in range(TT):
                        n = TT * h + t
                        act.wait_ge(r_mvd, n + 1)
                        act.activation(r_sd[:, n, :], r_mv[:, n, 1:2], ACT.Sqrt, bias=eps[:, 0:1]).then_inc(r_sdd, 1)

                def hi(h):
                    for b in range(2):
                        act.wait_ge(turn_full, ph.turn + 2 * TT + 2 * h + b + 1)
                        for j in range(2):
                            k = 4 * h + 2 * b + j
                            dst = xT_hi if k < KD else zT_hi
                            last = act.activation(dst[:, k % KD, :], turn[:, b, j * SEQ:(j + 1) * SEQ], ACT.Copy,
                                                  scale=nw[:, 104 + k:105 + k])
                        last.then_inc(turn_hi, 1)

                for h in range(RH + 2):
                    if h < RH:
                        turned(h)
                    if 1 <= h <= RH:
                        deviations(h - 1)
                    if h >= 2:
                        hi(h - 2)
                mixer_out(ph)

            for n in range(4):
                split_hi(act, n)
            act.wait_ge(nw_ready, 1)
            act.wait_ge(eps_set, 1)
            for ph in phases:
                if ph.kind == "ffn":
                    ffn(ph, ph.n == len(phases) - 1)
                else:
                    {"attn": attn, "mlstm": mlstm, "ret": ret}[ph.kind](ph)
            for t in range(TT):
                statistics(len(phases), t)

        @block.vector
        def _(v):
            chain = [0]

            def link(ins):
                chain[0] += 1
                ins.then_inc(dve, 1)
                v.wait_ge(dve, chain[0])

            def x_lo(ph, t):
                for half in range(2):
                    v.wait_ge(turn_hi, ph.turn + 2 * t + half + 1)
                    for k in range(4):
                        f = 4 * half + k
                        last = v.scalar_tensor_tensor(xT_lo[:, f, t * P:(t + 1) * P], turn[:, half, k * P:(k + 1) * P],
                                                      nw[:, norm_col(ph) + f:norm_col(ph) + f + 1],
                                                      xT_hi[:, f, t * P:(t + 1) * P].bitcast(F32),
                                                      ALU.mult, ALU.subtract)
                    last.then_inc(turn_free, 1)

            def root(p, t):
                v.wait_ge(rms_done, TT * p + t + 1)
                v.reciprocal(rstd[:, t:t + 1], rms[:, t:t + 1]).then_inc(rstd_ready, 1)

            def add_x(ph, t, half):
                accumulated(v, ph, t, half)
                xq = xs[:, t, half * NB:(half + 1) * NB]
                v.scalar_tensor_tensor(xq, acc[:, 2 * t + half, :], 0.5 if ph.kind == "ffn" else 1.0, xq,
                                       ALU.mult, ALU.add).then_inc(x_ready, 1)

            def finish(ph):
                following = phases[ph.n + 1] if ph.n + 1 < len(phases) else None
                for t, half in ((0, 0), (0, 1), (1, 0)):
                    add_x(ph, t, half)
                if following:
                    x_lo(following, 0)
                add_x(ph, 1, 1)
                if following:
                    root(following.n, 0)
                    x_lo(following, 1)
                    root(following.n, 1)

            def hidden(ph, c, t):
                v.wait_ge(gate_done, count(TT * NCH * ph.ffn + t + 1, c, TT))
                v.scalar_tensor_tensor(f_hid[:, t, :], proj[:, t, CH:2 * CH], rstd[:, t:t + 1], f_gate[:, t, :],
                                       ALU.mult, ALU.mult).then_inc(proj_free, 1)

            def turned_lo(bank, k, threshold):
                v.wait_ge(turn_hi, threshold)
                v.tensor_tensor(zT_lo[:, k:k + 2, :].rearrange("p a b -> p (a b)"), turn[:, bank, :],
                                zT_hi[:, k:k + 2, :].rearrange("p a b -> p (a b)").bitcast(F32), ALU.subtract) \
                 .then_inc(turn_free, 1)

            def ffn(ph, final):
                v.wait_ge(rstd_ready, TT * ph.n + TT)
                hidden(ph, 0, 0)
                for q in range(3):
                    split_lo(v, ph.unit + 4 + q)
                hidden(ph, 0, 1)
                split_lo(v, ph.unit + 7)

                def chunk(c, ahead=4):
                    n = ph.unit + 2
                    split_lo(v, n, c)
                    split_lo(v, n + 1, c)
                    turned_lo(0, 0, count(ph.turn + 2 * TT, c, 1))
                    hidden(ph, c, 0)
                    for q in range(min(ahead, 3)):
                        split_lo(v, n + 2 + q, c)
                    hidden(ph, c, 1)
                    if ahead == 4:
                        split_lo(v, n + 5, c)

                chunk(1)
                with v.Fori(2, NCH - 1) as c:
                    chunk(c)
                chunk(NCH - 1, 2 if final else 4)
                turned_lo(1, 2, ph.turn + 2 * TT + NCH)
                if not final:
                    split_lo(v, ph.unit + 6 * NCH + 2)
                    split_lo(v, ph.unit + 6 * NCH + 3)
                finish(ph)

            def mixer_in(ph, n_chunks, evacuate, extra):
                v.wait_ge(rstd_ready, TT * ph.n + TT)
                for ch in range(n_chunks):
                    for t in range(TT):
                        projected(v, ph, ch, t)
                        evacuate(ch, t).then_inc(proj_free, 1)
                        for q in (range(3), [3])[t]:
                            split_lo(v, ph.unit + 4 * (ch + 1) + q)
                    if ch in extra:
                        extra[ch]()
                for q in range(2):
                    split_lo(v, ph.unit + 4 * (n_chunks + 1) + q)

            def mixer_out(ph):
                for i in range(KOUT[ph.kind] - 2):
                    split_lo(v, ph.unit + 4 * (PROJ[ph.kind] + 1) + 2 + i)

            def attn(ph):
                i = ph.mixer
                v.wait_ge(bias_in, 32 * (i + 1))
                mixer_in(ph, 3, lambda ch, t: v.scalar_tensor_tensor(
                    a_qkv[:, t, ch * NB:(ch + 1) * NB], proj[:, t, :], rstd[:, t:t + 1],
                    a_bias[:, ch * NB:(ch + 1) * NB], ALU.mult, ALU.add), {})
                for b in (1, 3, 5):
                    v.wait_ge(a_turned, 6 * i + b + 1)
                    dst = a_qT[:, 2 * b:2 * b + 2, :] if b < 4 else a_kT[:, 2:4, :]
                    src = acc[:, b, :] if b < 4 else turn[:, 1, :]
                    v.tensor_copy(dst.rearrange("p a b -> p (a b)"), src).then_inc(a_evac_v, 1)

                def maxima(g):
                    v.wait_ge(a_sfull, 4 * i + g + 1)
                    s = a_s[g % 2]
                    v.tensor_tensor(s[:, :, :], acc[:, 0:GRP, 0:TRI],
                                    const[:, C_MA:C_MA + TRI].rearrange("p (o m) -> p o m", o=1)
                                    .to_broadcast([P, GRP, TRI]), ALU.add).then_inc(a_masked, 1)
                    v.wait_ge(a_masked, 4 * i + g + 1)
                    for t in range(TT):
                        last = v.tensor_reduce(a_mx[:, g, t * GRP:(t + 1) * GRP], s[:, :, t * P:t * P + (t + 1) * P],
                                               AX, ALU.max)
                    link(last)
                    sink = sinks[:, i:i + 1, GRP * g:GRP * (g + 1)].to_broadcast([P, TT, GRP])
                    two = "p (t h) -> p t h"
                    link(v.scalar_tensor_tensor(a_m[:, g, :].rearrange(two, t=TT), a_mx[:, g, :].rearrange(two, t=TT),
                                                HD ** -0.5, sink, ALU.mult, ALU.max))
                    v.tensor_tensor(a_se[:, g, :].rearrange(two, t=TT), sink, a_m[:, g, :].rearrange(two, t=TT),
                                    ALU.subtract)
                    v.tensor_scalar(a_nm[:, g, :], a_m[:, g, :], -1.0, None, ALU.mult).then_inc(a_max, 1)

                def copies(g):
                    v.wait_ge(a_exp, 4 * i + g + 1)
                    link(v.tensor_tensor(a_den[:, g, :], a_sum[:, g, :], a_se[:, g, :], ALU.add))
                    link(v.reciprocal(a_rden[:, g, :], a_den[:, g, :]))
                    v.wait_ge(a_pfull, 3 * (4 * i + g) + 3)
                    v.tensor_copy(a_pT[g % 2][:, 2, :], turn[:, 0, :]).then_inc(a_pcopy_v, 1)

                def outputs(g):
                    v.wait_ge(a_ofull, 4 * i + g + 1)
                    v.tensor_tensor(
                        a_qkv[:, :, g * GRP * HD:(g + 1) * GRP * HD].rearrange("p t (h e) -> p t h e", e=HD),
                        turn[:, 1, :].rearrange("p (t h e) -> p t h e", t=TT, h=GRP),
                        a_rden[:, g, :].rearrange("p (t h o) -> p t h o", t=TT, o=1).to_broadcast([P, TT, GRP, HD]),
                        ALU.mult).then_inc(a_odone, 1)

                maxima(0)
                for g in range(KVH):
                    if g + 1 < KVH:
                        maxima(g + 1)
                    copies(g)
                    outputs(g)
                for b in range(4):
                    turned_lo(b % 2, 2 * b, ph.turn + 2 * TT + b + 1)
                mixer_out(ph)
                v.wait_ge(bo_added, i + 1)
                finish(ph)

            def mlstm(ph):
                def evacuate(ch, t):
                    r = rstd[:, t:t + 1]
                    if ch < 2:
                        return v.tensor_scalar(m_qk[:, t, ch * NB:(ch + 1) * NB], proj[:, t, :], r, None, ALU.mult)
                    if ch < 4:
                        h = t * MH + 4 * (ch - 2)
                        return v.tensor_scalar(m_v[:, h:h + 4, 0:MDV], proj[:, t, :].rearrange("p (h e) -> p h e", h=4),
                                               r, None, ALU.mult)
                    return v.tensor_scalar(m_o[:, t, (ch - 4) * NB:(ch - 3) * NB], proj[:, t, :], r, None, ALU.mult)

                def gates():
                    v.wait_ge(m_gfull, 1)
                    for t in range(TT):
                        last = v.scalar_tensor_tensor(m_g[:, t, :], turn[:, 0, t * 2 * MH:(t + 1) * 2 * MH],
                                                      rstd[:, t:t + 1], bgate[:, :], ALU.mult, ALU.add)
                    last.then_inc(m_graw, 1)

                def rows():
                    v.wait_ge(m_rfull, 1)
                    r8 = slice(0, MH)
                    link(v.tensor_tensor_scan(m_C[r8, :], const[r8, C_ONE:C_ONE + SEQ], turn[r8, 1, SEQ:2 * SEQ], 0.0,
                                              ALU.mult, ALU.add))
                    link(v.scalar_tensor_tensor(m_a[r8, :], turn[r8, 1, 0:SEQ], CAP, m_C[r8, :], ALU.mult, ALU.add))
                    link(v.tensor_tensor_scan(m_M[r8, :], m_a[r8, :], m_a[r8, :], 0.0, ALU.max, ALU.max))
                    v.tensor_tensor(m_cm[r8, :], m_C[r8, :], m_M[r8, :], ALU.subtract).then_inc(m_rows, 1)

                def columns():
                    v.wait_ge(m_emd, 1)
                    v.tensor_copy(m_acol[:, :, :].rearrange("p a b -> p (a b)"), turn[:, 0, 0:2 * MH]) \
                     .then_inc(m_cols, 1)

                mixer_in(ph, 6, evacuate, {0: gates, 3: rows})
                columns()

                def shifted(h):
                    v.wait_ge(m_sfull, h + 1)
                    v.tensor_tensor(m_w[h % 2], const[:, C_MB:C_MB + TRI], acc[:, 2 + h % 2, 0:TRI],
                                    ALU.subtract).then_inc(m_wpre, 1)

                def weighted(h):
                    v.wait_ge(m_wexp, h + 1)
                    v.tensor_tensor(m_p[h % 2], acc[:, h % 2, 0:TRI], m_w[h % 2], ALU.mult).then_inc(m_pdone, 1)

                def copies(h):
                    v.wait_ge(m_ssd, h + 1)
                    v.tensor_copy(m_num[:, TT * h:TT * (h + 1), :].rearrange("p a b -> p (a b)"),
                                  proj[:, h % 2, 0:TT * (MDV + 1)]).then_inc(m_ycopy, 1)

                shifted(0)
                for h in range(MH):
                    if h + 1 < MH:
                        shifted(h + 1)
                    weighted(h)
                    if h:
                        copies(h - 1)
                copies(MH - 1)
                v.wait_ge(m_ycopy, MH)
                nq = m_num[:, :, MDV].rearrange("p (h t) -> p t h", t=TT)
                link(v.scalar_tensor_tensor(m_den[:, :, :], nq, -1.0, nq, ALU.mult, ALU.max))
                link(v.tensor_tensor(m_den[:, :, :], m_den[:, :, :], m_em[:, :, :], ALU.max))
                link(v.reciprocal(m_rd[:, :, :], m_den[:, :, :]))
                link(v.tensor_tensor(m_t[:, :, :], m_ss[:, :, :], m_rd[:, :, :], ALU.mult))
                v.tensor_tensor(m_t[:, :, :], m_t[:, :, :], m_rd[:, :, :], ALU.mult).then_inc(m_var, 1)
                v.wait_ge(m_root, 1)
                link(v.reciprocal(m_fs[:, :, :], m_rs[:, :, :]))
                link(v.tensor_tensor(m_fs[:, :, :], m_fs[:, :, :], m_rd[:, :, :], ALU.mult))
                v.wait_ge(m_sig, 1)
                for h in range(MH):
                    for t in range(TT):
                        o = m_o[:, t, h * MDV:(h + 1) * MDV]
                        last = v.scalar_tensor_tensor(o, m_num[:, TT * h + t, 0:MDV], m_fs[:, t, h:h + 1], o,
                                                      ALU.mult, ALU.mult)
                    last.then_inc(m_y, 1)
                for b in range(4):
                    v.wait_ge(turn_hi, ph.turn + 2 * TT + b + 1)
                    for j in range(2):
                        k = 2 * b + j
                        last = v.scalar_tensor_tensor(zT_lo[:, k, :], turn[:, b % 2, j * SEQ:(j + 1) * SEQ],
                                                      nw[:, 96 + k:97 + k], zT_hi[:, k, :].bitcast(F32),
                                                      ALU.mult, ALU.subtract)
                    last.then_inc(turn_free, 1)
                mixer_out(ph)
                finish(ph)

            def ret(ph):
                def evacuate(ch, t):
                    return v.tensor_scalar(r_all[:, t, ch * NB:(ch + 1) * NB], proj[:, t, :], rstd[:, t:t + 1], None,
                                           ALU.mult)

                def rotate(ch):
                    v.wait_ge(proj_free, ph.group + 2 * ch + 2)
                    for t in range(TT):
                        x_ = r_all[:, t, ch * NB:(ch + 1) * NB].rearrange("p (h e two) -> p h two e", h=2, two=2)
                        x1, x2 = x_[:, :, 0, :], x_[:, :, 1, :]
                        co = cos[:, t:t + 1, ROPE_HALF:N_INV].to_broadcast([P, 2, P])
                        si = sin[:, t:t + 1, ROPE_HALF:N_INV].to_broadcast([P, 2, P])
                        tm = [r_tmp[:, j, :].rearrange("p (h e) -> p h e", h=2) for j in range(4)]
                        v.tensor_tensor(tm[0], x1, co, ALU.mult)
                        v.tensor_tensor(tm[1], x2, si, ALU.mult)
                        v.tensor_tensor(tm[2], x2, co, ALU.mult)
                        link(v.tensor_tensor(tm[3], x1, si, ALU.mult))
                        v.tensor_tensor(x1, tm[0], tm[1], ALU.subtract)
                        v.tensor_tensor(x2, tm[2], tm[3], ALU.add).then_inc(r_rot, 1)
                        v.wait_ge(r_rot, TT * ch + t + 1)

                mixer_in(ph, 12, evacuate, {c + 2: (lambda c=c: rotate(c)) for c in range(4)})

                def decayed(h):
                    v.wait_ge(r_sfull, h + 1)
                    v.tensor_tensor(r_p[h % 2], acc[:, 2, 0:TRI], const[:, C_DM + h * TRI:C_DM + (h + 1) * TRI],
                                    ALU.mult).then_inc(r_pdone, 1)

                def normed(h):
                    banks = [acc[:, 3, :], proj[:, 0, :]]
                    for t in range(TT):
                        n = TT * h + t
                        v.wait_ge(r_yfull, n + 1)
                        link(v.bn_stats(r_bn[:, n, :], banks[t]))
                        v.bn_aggr(r_mv[:, n, :], r_bn[:, n, :]).then_inc(r_mvd, 1)
                    for t in range(TT):
                        n = TT * h + t
                        v.wait_ge(r_sdd, n + 1)
                        link(v.reciprocal(r_rs[:, n, :], r_sd[:, n, :]))
                        if n >= 2:
                            v.wait_ge(r_gated, n - 1)
                        v.tensor_scalar(r_y[n % 2], banks[t], r_mv[:, n, 0:1], r_rs[:, n, :], ALU.subtract,
                                        ALU.mult).then_inc(r_norm, 1)

                def lo(h):
                    for b in range(2):
                        v.wait_ge(turn_hi, ph.turn + 2 * TT + 2 * h + b + 1)
                        for j in range(2):
                            k = 4 * h + 2 * b + j
                            hi, dst = (xT_hi, xT_lo) if k < KD else (zT_hi, zT_lo)
                            last = v.scalar_tensor_tensor(dst[:, k % KD, :], turn[:, b, j * SEQ:(j + 1) * SEQ],
                                                          nw[:, 104 + k:105 + k], hi[:, k % KD, :].bitcast(F32),
                                                          ALU.mult, ALU.subtract)
                        last.then_inc(turn_free, 1)

                for h in range(RH + 2):
                    if h < RH:
                        decayed(h)
                    if 1 <= h <= RH:
                        normed(h - 1)
                    if h >= 2:
                        lo(h - 2)
                mixer_out(ph)
                finish(ph)

            for n in range(4):
                split_lo(v, n)
            v.wait_ge(nw_turned, 1)
            v.tensor_copy(nw[:, 0:120], acc[:, 0, 0:120]).then_inc(nw_ready, 1)
            v.wait_ge(nw_ready, 1)
            x_lo(phases[0], 0)
            root(0, 0)
            x_lo(phases[0], 1)
            root(0, 1)
            for ph in phases:
                if ph.kind == "ffn":
                    ffn(ph, ph.n == len(phases) - 1)
                else:
                    {"attn": attn, "mlstm": mlstm, "ret": ret}[ph.kind](ph)
            v.wait_ge(final_in, 16)
            for t in range(TT):
                root(len(phases), t)
                v.wait_ge(rstd_ready, TT * len(phases) + t + 1)
                v.scalar_tensor_tensor(xs[:, t, :], xs[:, t, :], rstd[:, t:t + 1], final_w, ALU.mult, ALU.mult) \
                 .then_inc(x_ready, 1)


_INS = ['x', 'positions', 'norm_w', 'final_norm_w', 'ffn_w_in', 'ffn_w_out', 'attn_w_qkv', 'attn_b_qkv', 'attn_w_o',
        'attn_b_o', 'attn_sinks', 'mlstm_w_in', 'mlstm_b_if', 'mlstm_norm_w', 'mlstm_w_out', 'ret_w_in', 'ret_norm_w',
        'ret_w_out']


def kernel(**inputs):
    import concourse.bacc as _bacc
    from concourse.bass_utils import run_bass_kernel_spmd as _run

    nc = _bacc.Bacc("TRN2", target_bir_lowering=False, num_devices=1)
    arrays, args = {}, []
    given = {name: np.ascontiguousarray(inputs[name]) for name in _INS}
    given["consts"] = constants()
    for name, a in given.items():
        arrays[f"in_{name}"] = a
        args.append(nc.dram_tensor(f"in_{name}", a.shape, mybir.dt.from_np(a.dtype), kind="ExternalInput").ap())
    args.append(nc.dram_tensor("out_0", (1, SEQ, D), F32, kind="ExternalOutput").ap())
    build(nc, *args)
    r = _run(nc, [arrays], core_ids=[0])
    return r.results[0]["out_0"]
```

```python
from contextlib import ExitStack

import numpy as np

import concourse.bass as bass
from concourse import mybir

F32 = mybir.dt.float32
F32R = mybir.dt.float32r
I32 = mybir.dt.int32
ALU = mybir.AluOpType
ACT = mybir.ActivationFunctionType
AX = mybir.AxisListType.X

P = 128
D = 1024
SEQ = 256
TT = SEQ // P
KD = D // P
FF = 2816
CH = 256
NCH = FF // CH
NB = 512
EPS = 1e-6
RING = 6
U = 1024
NEG = -1e30

HEADS, KVH, HD = 16, 4, 64
GRP = HEADS // KVH
ROPE_HALF = HD // 8
MH, MDK, MDV = 8, 64, 128
CAP = 15.0
RH, RDK, RDV = 4, 256, 512
TRI = 3 * P

COLUMNS = {"attn": (2, 0, 1), "mlstm": tuple(range(6)), "ret": (0, 2, 1, 3, *range(4, 12))}
PHASES = ["ffn", "attn", "ffn", "ffn", "mlstm", "ffn", "ffn", "ret", "ffn", "ffn", "attn", "ffn"]
PROJ = {"ffn": NCH, "attn": 3, "mlstm": 6, "ret": 12}
KOUT = {"ffn": 2 * NCH, "attn": 8, "mlstm": 8, "ret": 16}
TURNS = {"ffn": NCH, "attn": 8, "mlstm": 4, "ret": 8}

N_ROWS = KD * len(PHASES)
ALL_ROWS = N_ROWS + MH * MDV // P + RH * RDV // P

C_ID = 0
C_MA = C_ID + P
C_MB = C_MA + TRI
C_DM = C_MB + TRI
C_SEL = C_DM + RH * TRI
C_INV = C_SEL + MH * P
N_INV = ROPE_HALF + RDK // 2
C_ONE = C_INV + N_INV
N_CONST = C_ONE + SEQ


class Phase:

    def __init__(self, n, kind, unit, group, turn, ffn, mixer):
        self.n, self.kind, self.unit, self.group, self.turn = n, kind, unit, group, turn
        self.ffn, self.mixer = ffn, mixer


def plan():
    out, unit, group, turn, seen = [], 0, 0, 0, {}
    for n, kind in enumerate(PHASES):
        i = seen.get(kind, 0)
        seen[kind] = i + 1
        out.append(Phase(n, kind, unit, group, turn, i, i))
        unit += 4 * PROJ[kind] + KOUT[kind]
        group += TT * PROJ[kind]
        turn += 2 * TT + TURNS[kind]
    return out, unit


def constants():
    c = np.zeros((P, N_CONST), np.float32)
    c[:, C_ID:C_ID + P] = np.eye(P)
    i = np.arange(P)
    row, col = i[:, None], i[None, :]
    c[:, C_MA:C_MA + P] = np.where(col <= row, 0, NEG)
    c[:, C_MA + P:C_MA + 2 * P] = np.where(col > row, 0, NEG)
    c[:, C_MA + 2 * P:C_MA + 3 * P] = np.where(col <= row, 0, NEG)
    c[:, C_MB:C_MB + P] = np.where(col >= row, 0, NEG)
    c[:, C_MB + 2 * P:C_MB + 3 * P] = np.where(col >= row, 0, NEG)
    for h in range(RH):
        log_gamma = np.log1p(-2.0 ** (-5.0 - h))
        for b, away in ((0, 0), (1, P), (2, 0)):
            diff = col + away - row
            at = C_DM + h * TRI + b * P
            c[:, at:at + P] = np.where(diff >= 0, np.exp(np.maximum(diff, 0) * log_gamma), 0) * RDK ** -0.5
    for h in range(MH):
        c[h, C_SEL + h * P:C_SEL + (h + 1) * P] = 1
    rope = 1.0 / 500000.0 ** (np.arange(0, 2 * ROPE_HALF, 2) / (2.0 * ROPE_HALF))
    ret = 1.0 / 10000.0 ** np.linspace(0.0, 1.0, RDK // 2)
    c[:, C_INV:C_INV + N_INV] = np.concatenate([rope, ret])
    c[:, C_ONE:] = 1
    return c


def build(nc, x, positions, norm_w, final_norm_w, ffn_w_in, ffn_w_out, attn_w_qkv, attn_b_qkv, attn_w_o,
          attn_b_o, attn_sinks, mlstm_w_in, mlstm_b_if, mlstm_norm_w, mlstm_w_out, ret_w_in, ret_norm_w,
          ret_w_out, consts, out):
    phases, n_units = plan()
    ctx = ExitStack()
    with ctx:
        def sb(name, shape, dt=F32):
            return ctx.enter_context(nc.sbuf_tensor(name, shape, dt))

        def sem(name):
            return ctx.enter_context(nc.semaphore(name))

        const = sb("const", [P, N_CONST])
        ident = const[:, C_ID:C_ID + P]
        xs = sb("xs", [P, TT, D])
        xT_hi = sb("xT_hi", [P, KD, SEQ], F32R)
        xT_lo = sb("xT_lo", [P, KD, SEQ], F32R)
        zT_hi = sb("zT_hi", [P, KD, SEQ], F32R)
        zT_lo = sb("zT_lo", [P, KD, SEQ], F32R)
        raw = sb("raw", [P, RING, U])
        w_hi = sb("w_hi", [P, RING, U], F32R)
        w_lo = sb("w_lo", [P, RING, U], F32R)
        nw_rows = sb("nw_rows", [P, P])
        nw = sb("nw", [P, P])
        pos_i = sb("pos_i", [P, TT], I32)
        pos_f = sb("pos_f", [P, TT])
        cos = sb("cos", [P, TT, N_INV])
        sin = sb("sin", [P, TT, N_INV])
        sinks = sb("sinks", [P, 2, HEADS])
        wgate = sb("wgate", [P, KD, 2 * MH])
        wg_hi = sb("wg_hi", [P, KD, P], F32R)
        wg_lo = sb("wg_lo", [P, KD, P], F32R)
        bgate = sb("bgate", [P, 2])
        sel = sb("sel", [MH, MH * P], F32R)
        M_hi = sb("M_hi", [MH, SEQ], F32R)
        M_lo = sb("M_lo", [MH, SEQ], F32R)
        ssq = sb("ssq", [P, TT])
        rms = sb("rms", [P, TT])
        rstd = sb("rstd", [P, TT])
        eps = sb("eps", [P, 1])
        warm = sb("warm", [P, 1])
        ARENA = 15900
        arena = sb("arena", [P, ARENA])

        acc = ctx.enter_context(nc.psum_tensor("acc", [P, 4, NB], F32))
        proj = ctx.enter_context(nc.psum_tensor("proj", [P, TT, NB], F32))
        turn = ctx.enter_context(nc.psum_tensor("turn", [P, 2, NB], F32))

        def carve(*shapes):
            at, views = 0, []
            for shape in shapes:
                n = int(np.prod(shape))
                v = arena[:, at:at + n]
                if len(shape) == 2:
                    v = v.rearrange("p (a b) -> p a b", a=shape[0])
                if len(shape) == 3:
                    v = v.rearrange("p (a b c) -> p a b c", a=shape[0], b=shape[1])
                views.append(v)
                at += n
            assert at <= ARENA, at
            return views

        f_gate, f_hid = carve((TT, CH), (TT, CH))
        _, t_ang, t_k, t_r, t_p, final_w = carve((2 * TT * CH,), *[(TT, N_INV)] * 4, (D,))
        (a_qkv, a_bias, a_bo, a_qT, a_kT, a_s0, a_s1, a_pT0, a_pT1, a_rot, a_kdup, a_nsink, a_mx, a_nm, a_se, a_sum, a_den,
         a_rden) = carve((TT, 1536), (1536,), (D,), (8, SEQ), (KVH, SEQ), (2, TRI), (2, TRI), (2 * TRI,), (2 * TRI,),
                         (4, 8 * ROPE_HALF), (TT, 2 * KVH * HD), (HEADS,), *[(HEADS // 2, 4)] * 6)
        a_s, a_pT = [a_s0, a_s1], [a_pT0, a_pT1]
        (m_qk, m_v, m_o, m_qT, m_kT, m_w0, m_w1, m_p0, m_p1, m_num, m_diag, m_R, m_g, m_th, m_e, m_nl, m_C, m_a, m_M, m_cm,
         m_acol, m_em, m_ss, m_den, m_rd, m_t, m_rs, m_fs, m_sq) = carve(
            (TT, 1024), (TT * MH, MDV + 1), (TT, 1024), (4, SEQ), (4, SEQ), (TRI,), (TRI,), (TRI,), (TRI,),
            (MH * TT, MDV + 1), (SEQ,), (SEQ,), (SEQ,), (SEQ,), (SEQ,), (SEQ,), (SEQ,), (SEQ,), (SEQ,), (SEQ,),
            *[(TT, MH)] * 8, (TT, MDV))
        m_w, m_p = [m_w0, m_w1], [m_p0, m_p1]
        (r_qkv, r_tmp, r_qk0, r_qk1, r_p0, r_p1, r_gate, r_bn, r_mv, r_sd, r_rs) = carve(
            (TT, 4096), (4, 256), (2, 2 * SEQ), (2, 2 * SEQ), (TRI,), (TRI,), (TT, NB), (RH * TT, 6),
            (RH * TT, 2), (RH * TT, 1), (RH * TT, 1))
        r_qk, r_p = [r_qk0, r_qk1], [r_p0, r_p1]

        raw_in = [sem(f"raw_in{i}") for i in range(RING)]
        hi_done = sem("hi_done")
        split_done = sem("split_done")
        unit_used = sem("unit_used")
        proj_full = sem("proj_full")
        gate_done = sem("gate_done")
        proj_free = sem("proj_free")
        turn_full = sem("turn_full")
        turn_hi = sem("turn_hi")
        turn_free = sem("turn_free")
        acc_full = sem("acc_full")
        x_ready = sem("x_ready")
        x_in = [sem(f"x_in{t}") for t in range(TT)]
        ssq_done = sem("ssq_done")
        rms_done = sem("rms_done")
        rstd_ready = sem("rstd_ready")
        const_in = sem("const_in")
        tables_in = sem("tables_in")
        rows_in = sem("rows_in")
        own_rows_in = sem("own_rows_in")
        nw_turned = sem("nw_turned")
        nw_ready = sem("nw_ready")
        eps_set = sem("eps_set")
        angles_ready = sem("angles_ready")
        sincos = sem("sincos")
        dve = sem("dve")
        pool = sem("pool")
        bias_in = sem("bias_in")
        bo_added = sem("bo_added")
        roped = sem("roped")
        nsink = sem("nsink")
        a_turned = sem("a_turned")
        a_evac_a = sem("a_evac_a")
        a_evac_v = sem("a_evac_v")
        a_sfull = sem("a_sfull")
        a_masked = sem("a_masked")
        a_max = sem("a_max")
        a_exp = sem("a_exp")
        a_normed = sem("a_normed")
        a_pfull = sem("a_pfull")
        a_pcopy_a = sem("a_pcopy_a")
        a_pcopy_v = sem("a_pcopy_v")
        m_ones = sem("m_ones")
        gate_w = sem("gate_w")
        m_dready = sem("m_dready")
        m_gfull = sem("m_gfull")
        m_graw = sem("m_graw")
        m_act = sem("m_act")
        m_rows = sem("m_rows")
        m_cfull = sem("m_cfull")
        m_cols = sem("m_cols")
        m_emd = sem("m_emd")
        m_turned = sem("m_turned")
        m_tcopy = sem("m_tcopy")
        m_sfull = sem("m_sfull")
        m_wpre = sem("m_wpre")
        m_wexp = sem("m_wexp")
        m_pdone = sem("m_pdone")
        m_yfull = sem("m_yfull")
        m_ssd = sem("m_ssd")
        m_ycopy = sem("m_ycopy")
        m_var = sem("m_var")
        m_root = sem("m_root")
        m_sig = sem("m_sig")
        m_y = sem("m_y")
        r_rot = sem("r_rot")
        r_silu = sem("r_silu")
        r_turned = sem("r_turned")
        r_tcopy = sem("r_tcopy")
        r_sfull = sem("r_sfull")
        r_pdone = sem("r_pdone")
        r_yfull = sem("r_yfull")
        r_mvd = sem("r_mvd")
        r_sdd = sem("r_sdd")
        r_norm = sem("r_norm")
        final_in = sem("final_in")
        out_ready = sem("out_ready")
        out_done = sem("out_done")

        def slot(n):
            return n % RING

        def unit_threshold(n, c):
            return 16 * (n // RING + 1) + (c * 16 if not isinstance(c, int) else 16 * c)

        def count(base, c, step):
            return base + step * c if isinstance(c, int) else c * step + base

        def later(value, c, step):
            return value + step * (c if isinstance(c, int) else 2) > 0

        def split_hi(act, n, c=0):
            act.wait_ge(raw_in[slot(n)], unit_threshold(n, c))
            if later(n - RING + 1, c, RING):
                act.wait_ge(unit_used, count(n - RING + 1, c, RING))
            act.activation(w_hi[:, slot(n), :], raw[:, slot(n), :], ACT.Copy).then_inc(hi_done, 1)

        def split_lo(v, n, c=0):
            v.wait_ge(hi_done, count(n + 1, c, RING))
            v.tensor_tensor(w_lo[:, slot(n), :], raw[:, slot(n), :], w_hi[:, slot(n), :].bitcast(F32),
                            ALU.subtract).then_inc(split_done, 1)

        def projected(eng, ph, c, t):
            if t == 0:
                eng.wait_ge(proj_full, count(ph.group // 2 + 1, c, 1))
            elif ph.kind == "ffn" and not (isinstance(c, int) and c == 0):
                eng.wait_ge(unit_used, count(ph.unit + 2, c, RING))
            else:
                eng.wait_ge(unit_used, ph.unit + 4 * (c + 1))

        M_FROM = 2
        M_STEP = 2
        R_HEAD = 5
        R_GATE = 8

        def m_quarters():
            return [(s, M_FROM + 1 + s // 8, s % 8) for s in range(-8, 8 * (PROJ["mlstm"] - M_FROM - 1))]

        def m_head(s):
            return s // M_STEP if s > 0 and s % M_STEP == 1 and s // M_STEP < MH else None

        def split_ahead(split, eng, ph, c, place):
            if place in (0, 2, 5, 6):
                split(eng, ph.unit + 4 * (c + 1) + (0, 2, 5, 6).index(place))

        def accumulated(eng, ph, t, half):
            if t == 0 or half == 0:
                eng.wait_ge(acc_full, 3 * ph.n + 2 * t + half + 1)
            else:
                eng.wait_ge(unit_used, ph.unit + 4 * PROJ[ph.kind] + KOUT[ph.kind])

        def x_wait(eng, p, t, half):
            if p == 0:
                eng.wait_ge(x_in[t], 16)
            else:
                eng.wait_ge(x_ready, 4 * (p - 1) + 2 * t + half + 1)

        def norm_col(ph):
            return ph.n * KD

        block = ctx.enter_context(nc.Block())

        @block.sync
        def _(sp):
            def load(n, c, dst, src):
                if later(n - RING + 1, c, RING):
                    sp.wait_ge(split_done, count(n - RING + 1, c, RING))
                sp.dma_start(dst, src).then_inc(raw_in[slot(n)], 16)

            def ffn_in(ph, n, c, chunk, units=range(4)):
                w = ffn_w_in[ph.ffn // 2, ph.ffn % 2].rearrange("(k p) (g m) -> p k g m", p=P, g=2)
                for q in units:
                    load(n + q, c, raw[:, slot(n + q), :].rearrange("p (k m) -> p k m", k=4),
                         w[:, q // 2 * 4:q // 2 * 4 + 4, q % 2, bass.ds(chunk * CH, CH)])

            def ffn_out(ph, n, c, chunk):
                w = ffn_w_out[ph.ffn // 2, ph.ffn % 2].rearrange("(j k p) m -> p j k m", p=P, k=2)
                for k in range(2):
                    load(n + k, c, raw[:, slot(n + k), :], w[:, chunk, k, :])

            for t in range(TT):
                sp.dma_start(xs[:, t, :], x[0, t * P:(t + 1) * P, :]).then_inc(x_in[t], 16)
                ffn_in(phases[0], 0, 0, 0, (2 * t, 2 * t + 1))
            for ph in phases:
                if ph.kind == "ffn":
                    if ph.n:
                        ffn_in(ph, ph.unit, 0, 0)

                    def chunk(c):
                        ffn_in(ph, ph.unit - 2, c, c)
                        ffn_out(ph, ph.unit + 2, c, c - 1)

                    chunk(1)
                    with sp.Fori(2, NCH) as c:
                        chunk(c)
                    ffn_out(ph, ph.unit + 6 * NCH - 2, 0, NCH - 1)
                    continue
                w_in, w_out = {"attn": (attn_w_qkv, attn_w_o), "mlstm": (mlstm_w_in, mlstm_w_out),
                               "ret": (ret_w_in, ret_w_out)}[ph.kind]
                wi = w_in[ph.mixer].rearrange("(k p) m -> p k m", p=P)
                wo = w_out[ph.mixer].rearrange("(k p) m -> p k m", p=P)
                for ch in range(PROJ[ph.kind]):
                    at = NB * COLUMNS[ph.kind][ch]
                    for q in range(4):
                        n = ph.unit + 4 * ch + q
                        load(n, 0, raw[:, slot(n), :].rearrange("p (k m) -> p k m", k=2),
                             wi[:, 2 * q:2 * q + 2, at:at + NB])
                for k in range(KOUT[ph.kind]):
                    n = ph.unit + 4 * PROJ[ph.kind] + k
                    load(n, 0, raw[:, slot(n), :], wo[:, k, :])
            for t in range(TT):
                for half in range(2):
                    sp.wait_ge(out_ready, 2 * t + half + 1)
                    cols = slice(half * NB, (half + 1) * NB)
                    sp.dma_start(out[0, t * P:(t + 1) * P, cols], xs[:, t, cols]).then_inc(out_done, 16)
            sp.wait_ge(out_done, 16 * 2 * TT)

        @block.gpsimd
        def _(g):
            chain = [0]

            def link(ins):
                chain[0] += 1
                ins.then_inc(pool, 1)
                g.wait_ge(pool, chain[0])

            g.memset(eps[:], EPS).then_inc(eps_set, 1)
            g.dma_start(nw_rows[N_ROWS:N_ROWS + 8, :], mlstm_norm_w.rearrange("o (k f) -> (o k) f", f=P)) \
             .then_inc(own_rows_in, 16)
            g.dma_start(nw_rows[N_ROWS + 8:N_ROWS + 24, :], ret_norm_w.rearrange("o (k f) -> (o k) f", f=P)) \
             .then_inc(own_rows_in, 16)
            g.wait_ge(hi_done, 4)
            g.dma_start(const[:, P:N_CONST], consts[:, P:N_CONST]).then_inc(tables_in, 16)
            g.dma_start(pos_i[:, :], positions[0].rearrange("(t p) -> p t", p=P),
                        allow_slow_non_contiguous=True).then_inc(tables_in, 16)
            g.dma_start(sinks[:, :, :], attn_sinks.rearrange("(o s) h -> o s h", o=1).to_broadcast([P, 2, HEADS])) \
                .then_inc(tables_in, 16)
            g.dma_start(wgate[:, :, :], mlstm_w_in[0].rearrange("(k p) m -> p k m", p=P)[:, :, 3072:3088]) \
                .then_inc(tables_in, 16)
            b_if = mlstm_b_if.rearrange("o (g p) -> g p o", p=MH)
            for j in range(2):
                g.dma_start(bgate[j * 32:j * 32 + MH, 0:1], b_if[j]).then_inc(tables_in, 16)

            def angles():
                two_pi = 2 * np.pi
                magic = 1.5 * 2.0 ** 23
                parts, rest = [], two_pi
                for scale in (2.0 ** 5, 2.0 ** 13, 2.0 ** 21):
                    part = np.floor(rest * scale) / scale
                    parts.append(part)
                    rest -= part
                parts.append(rest)
                g.wait_ge(tables_in, 16 * 6)
                link(g.tensor_copy(pos_f[:, :], pos_i[:, :]))
                for t in range(TT):
                    last = g.tensor_scalar(t_ang[:, t, :], const[:, C_INV:C_INV + N_INV], pos_f[:, t:t + 1], None,
                                           ALU.mult)
                link(last)
                limit = float(np.nextafter(np.float32(np.pi), np.float32(0)))
                for j, dst in enumerate((t_r, t_k)):
                    turns = cos
                    link(g.tensor_scalar(turns[:, :, :], t_ang, 1 / two_pi, 0.25 * j, ALU.mult, ALU.add))
                    link(g.tensor_scalar(turns[:, :, :], turns[:, :, :], magic, None, ALU.add))
                    link(g.tensor_scalar(turns[:, :, :], turns[:, :, :], magic, None, ALU.subtract))
                    src = t_ang
                    for part in parts:
                        link(g.tensor_scalar(t_p, turns[:, :, :], float(part), None, ALU.mult))
                        link(g.tensor_tensor(dst, src, t_p, ALU.subtract))
                        src = dst
                    if j:
                        link(g.tensor_scalar(dst, dst, float(np.pi / 2), None, ALU.add))
                    ins = g.tensor_scalar(dst, dst, limit, -limit, ALU.min, ALU.max)
                    link(ins) if not j else ins.then_inc(angles_ready, 1)

            def gate_weights():
                g.wait_ge(tables_in, 16 * 6)
                link(g.memset(wg_lo[:, :, :].bitcast(F32), 0.0))
                link(g.memset(wg_hi[:, :, :].bitcast(F32), 0.0))
                pair = [slice(j * 32, j * 32 + MH) for j in range(2)]
                for j in range(2):
                    link(g.tensor_copy(wg_hi[:, :, pair[j]], wgate[:, :, j * MH:(j + 1) * MH]))
                    link(g.tensor_tensor(wg_lo[:, :, pair[j]], wgate[:, :, j * MH:(j + 1) * MH],
                                         wg_hi[:, :, pair[j]].bitcast(F32), ALU.subtract))
                    link(g.tensor_scalar(bgate[pair[j], 1:2], bgate[pair[j], 0:1], 1 / CAP, None, ALU.mult))
                g.tensor_copy(sel[:, :], const[0:MH, C_SEL:C_SEL + MH * P]).then_inc(gate_w, 1)

            angles()
            gate_weights()

            def attn(ph):
                i = ph.mixer
                g.wait_ge(x_ready, 4 * ph.n)
                g.wait_ge(sincos, 2)
                g.dma_start(a_bias, attn_b_qkv[i:i + 1, :].to_broadcast([P, 1536])).then_inc(bias_in, 16)
                g.dma_start(a_bo, attn_b_o[i:i + 1, :].to_broadcast([P, D])).then_inc(bias_in, 16)
                g.wait_ge(bias_in, 32 * (i + 1))
                g.tensor_scalar(a_nsink, sinks[:, i, :], -1.0, None, ALU.mult).then_inc(nsink, 1)
                for ch, column, nh in ((0, 2, 4), (1, 0, 8), (2, 1, 8)):
                    for t in range(TT):
                        g.wait_ge(proj_free, ph.group + 2 * ch + t + 1)
                        v = a_qkv[:, t, column * NB:column * NB + nh * HD].rearrange("p (h e) -> p h e", e=HD)
                        rot = [a_rot[:, j, 0:nh * ROPE_HALF].rearrange("p (h e) -> p h e", h=nh) for j in range(4)]
                        x1, x2 = v[:, :, 0:ROPE_HALF], v[:, :, ROPE_HALF:2 * ROPE_HALF]
                        co, si = (table[:, t:t + 1, 0:ROPE_HALF].to_broadcast([P, nh, ROPE_HALF])
                                  for table in (cos, sin))
                        g.tensor_tensor(rot[0], x1, co, ALU.mult)
                        g.tensor_tensor(rot[1], x2, si, ALU.mult)
                        g.tensor_tensor(rot[2], x2, co, ALU.mult)
                        link(g.tensor_tensor(rot[3], x1, si, ALU.mult))
                        g.tensor_tensor(x1, rot[0], rot[1], ALU.subtract)
                        last = g.tensor_tensor(x2, rot[2], rot[3], ALU.add)
                        if ch == 0:
                            link(last)
                            last = g.tensor_copy(
                                a_kdup[:, t, :].rearrange("p (h two e) -> p h two e", h=KVH, two=2),
                                v.rearrange("p h (o e) -> p h o e", o=1).to_broadcast([P, KVH, 2, HD]))
                        last.then_inc(roped, 1)
                        g.wait_ge(roped, TT * (3 * i + ch) + t + 1)
                for t in range(TT):
                    last = g.tensor_tensor(xs[:, t, :], xs[:, t, :], a_bo, ALU.add)
                last.then_inc(bo_added, 1)

            def mlstm(ph):
                g.wait_ge(x_ready, 4 * ph.n)
                g.memset(m_v[:, :, MDV:MDV + 1], 1.0).then_inc(m_ones, 1)

            for ph in phases:
                if ph.kind == "attn":
                    attn(ph)
                if ph.kind == "mlstm":
                    mlstm(ph)
            g.wait_ge(x_ready, 4 * (len(phases) - 1))
            g.dma_start(final_w, final_norm_w.rearrange("(o m) -> o m", o=1).to_broadcast([P, D])).then_inc(final_in, 16)

        @block.tensor
        def _(pe):
            def turn_x(p, t, half):
                x_wait(pe, p, t, half)
                for k in range(4):
                    f = (4 * half + k) * P
                    last = pe.transpose(turn[:, half, k * P:(k + 1) * P], xs[:, t, f:f + P], ident)
                last.then_inc(turn_full, 1)

            def three(dst, a, w, start, stop):
                pe.matmul(dst, a[0], w[0], start=start, stop=False)
                pe.matmul(dst, a[0], w[1], start=False, stop=False)
                return pe.matmul(dst, a[1], w[0], start=False, stop=stop)

            def project(ph, n, c, group, t, quarters=range(4), fills={}):
                gated = ph.kind == "ffn"
                for q in quarters:
                    if t == 0:
                        pe.wait_ge(split_done, count(n + q + (2 - q % 2 if gated else 1), c, RING))
                    if q == 0 and later(group - 1, c, TT):
                        pe.wait_ge(proj_free, count(group - 1, c, TT))
                    for k in (2 * q, 2 * q + 1):
                        if gated:
                            s = slot(n + q // 2 * 2)
                            w = [x_[:, s:s + 2, k % 4 * CH:(k % 4 + 1) * CH] for x_ in (w_hi, w_lo)]
                        else:
                            w = [x_[:, slot(n + q), k % 2 * NB:(k % 2 + 1) * NB] for x_ in (w_hi, w_lo)]
                        a = [x_[:, k, t * P:(t + 1) * P] for x_ in (xT_hi, xT_lo)]
                        last = three(proj[:, t, :], a, w, k == 0, k == KD - 1)
                    if t == 1 and (q % 2 or not gated):
                        last.then_inc(unit_used, 2 if gated else 1)
                    if q == 3 and t == 0:
                        last.then_inc(proj_full, 1)
                    if q in fills:
                        fills[q]()

            def first_chunk(ph, fills={}):
                for half in range(2):
                    pe.wait_ge(turn_free, ph.turn + 1 + half)
                    project(ph, ph.unit, 0, ph.group, 0, [2 * half])
                    if half == 0:
                        turn_x(ph.n, 1, 0)
                    project(ph, ph.unit, 0, ph.group, 0, [2 * half + 1])
                    if half == 0:
                        pe.wait_ge(turn_free, ph.turn + 2)
                        turn_x(ph.n, 1, 1)
                pe.wait_ge(turn_free, ph.turn + 4)
                project(ph, ph.unit, 0, ph.group + 1, 1, fills=fills)

            def out_pair(n, c, z, first, between=None):
                for k in range(2):
                    pe.wait_ge(split_done, count(n + k + 1, c, RING))
                    for t in range(TT):
                        for h in range(2):
                            w = [x_[:, slot(n + k), h * NB:(h + 1) * NB] for x_ in (w_hi, w_lo)]
                            a = [x_[:, z[k][1], t * P:(t + 1) * P] for x_ in z[k][0]]
                            last = three(acc[:, 2 * t + h, :], a, w, first and k == 0, False)
                    last.then_inc(unit_used, 1)
                    if k == 0 and between:
                        between()

            def out_last(ph, z, second=None):
                n = ph.unit + 4 * PROJ[ph.kind] + KOUT[ph.kind] - len(z)
                pe.wait_ge(split_done, n + len(z))
                for t in range(TT):
                    for h in range(2):
                        if t == 1 and ph.n + 1 < len(phases):
                            turn_x(ph.n + 1, 0, h)
                        for k in range(len(z)):
                            if second and t + h == 0 and k == 1:
                                second()
                            w = [x_[:, slot(n + k), h * NB:(h + 1) * NB] for x_ in (w_hi, w_lo)]
                            a = [x_[:, z[k][1], t * P:(t + 1) * P] for x_ in z[k][0]]
                            last = three(acc[:, 2 * t + h, :], a, w, False, k == len(z) - 1)
                            if t == 1 and h == 1:
                                last.then_inc(unit_used, 1)
                        if t == 0 or h == 0:
                            last.then_inc(acc_full, 1)

            def out_tile(n, z, t, first, halves):
                if t == 0:
                    pe.wait_ge(split_done, n + 1)
                for h in halves:
                    w = [x_[:, slot(n), h * NB:(h + 1) * NB] for x_ in (w_hi, w_lo)]
                    a = [x_[:, z[1], t * P:(t + 1) * P] for x_ in z[0]]
                    last = three(acc[:, 2 * t + h, :], a, w, first, False)
                if t == 1 and h == 1:
                    last.then_inc(unit_used, 1)

            def z_pair(k):
                return [((zT_hi, zT_lo), k), ((zT_hi, zT_lo), k + 1)]

            def turn_hidden(ph, c, bank):
                pe.wait_ge(proj_free, count(ph.group + 2, c, TT))
                for k in range(2):
                    for t in range(TT):
                        last = pe.transpose(turn[:, bank, k * SEQ + t * P:k * SEQ + (t + 1) * P],
                                            f_hid[:, t, k * P:(k + 1) * P], ident)
                last.then_inc(turn_full, 1)

            def ffn(ph):
                first_chunk(ph)
                tu = ph.turn + 2 * TT

                def chunk(c, first=False, last=False):
                    n = ph.unit - 2
                    project(ph, n, c, ph.group, 0)
                    turn_hidden(ph, c - 1, 0)
                    project(ph, n, c, ph.group + 1, 1)
                    pe.wait_ge(turn_free, count(tu, c, 1))
                    out_pair(n + 4, c, z_pair(0), first,
                             (lambda: turn_hidden(ph, c, 1)) if last else None)

                chunk(1, first=True)
                with pe.Fori(2, NCH - 1) as c:
                    chunk(c)
                chunk(NCH - 1, last=True)
                pe.wait_ge(turn_free, tu + NCH)
                out_last(ph, z_pair(2))

            def mixer_out(ph, pairs, between={}):
                n = ph.unit + 4 * PROJ[ph.kind]
                for i, z in enumerate(pairs):
                    last = i == len(pairs) - 1
                    pe.wait_ge(turn_free, ph.turn + 2 * TT + i + 1)
                    if last:
                        out_last(ph, z)
                    else:
                        out_pair(n + 2 * i, 0, z, i == 0, between.get(i))

            def attn(ph):
                i = ph.mixer
                pairs = HEADS // 2

                def turn_in(b):
                    pe.wait_ge(roped, TT * (3 * i + b // 2 + 1))
                    if b >= 4:
                        pe.wait_ge(a_masked, pairs * i + 2)
                    for j in range(2):
                        for t in range(TT):
                            dst = turn[:, b] if b < 2 else acc[:, 2 + b % 2]
                            if b < 2:
                                src = a_kdup[:, t, (2 * b + j) * P:(2 * b + j + 1) * P]
                            else:
                                src = a_qkv[:, t, (2 * (b - 2) + j) * P:(2 * (b - 2) + j + 1) * P]
                            last = pe.transpose(dst[:, j * SEQ + t * P:j * SEQ + (t + 1) * P], src, ident)
                    last.then_inc(a_turned, 1)

                def scores(s):
                    pe.wait_ge(a_evac_a, 3 * i + (2 if s < 4 else 3))
                    if s:
                        pe.wait_ge(a_evac_v, 3 * i + (2 if s < 6 else 3))
                    if s == 2:
                        pe.wait_ge(a_masked, pairs * i + 1)
                    if s == 3:
                        pe.wait_ge(proj_free, ph.group + 6)
                    if s > 3:
                        pe.wait_ge(a_masked, pairs * i + s)
                    for j in range(2):
                        for t in range(TT):
                            at = j * HD
                            bank = acc[:, s % 2 * 2 + j, :] if s < 3 else proj[:, j, :]
                            last = pe.matmul(bank[:, t * P:t * P + (t + 1) * P],
                                             a_qT[at:at + HD, s, t * P:(t + 1) * P],
                                             a_kT[at:at + HD, s // 2, 0:(t + 1) * P], start=True, stop=True)
                    last.then_inc(a_sfull, 1)

                def turn_p(s):
                    pe.wait_ge(a_normed, pairs * i + s + 1)
                    if s:
                        pe.wait_ge(turn_free, ph.turn + 2 * TT + s)
                    for b in range(3):
                        for j in range(2):
                            last = pe.transpose(turn[:, b // 2, (b % 2 * 2 + j) * P:(b % 2 * 2 + j + 1) * P],
                                                a_s[s % 2][:, j, b * P:(b + 1) * P], ident)
                        if b:
                            last.then_inc(a_pfull, 1)

                def values(s):
                    pe.wait_ge(a_pcopy_a, pairs * i + s + 1)
                    pe.wait_ge(a_pcopy_v, pairs * i + s + 1)
                    for t in range(TT):
                        for j in range(2):
                            dst = turn[j * HD:(j + 1) * HD, 1, SEQ + t * P:SEQ + (t + 1) * P]
                            kv = 1280 + s // 2 * HD
                            for k in range(t + 1):
                                at = (2 * (t + k) + j) * P
                                last = pe.matmul(dst, a_qkv[:, k, kv:kv + HD], a_pT[s % 2][:, at:at + P],
                                                 start=(k == 0), stop=(k == t))
                    last.then_inc(turn_full, 1)

                def out(s, t, halves=range(2)):
                    if s == 0 and t == 0:
                        pe.wait_ge(a_masked, pairs * i + 3)
                        pe.wait_ge(a_evac_a, 3 * (i + 1))
                        pe.wait_ge(a_evac_v, 3 * (i + 1))
                    if t == 0:
                        pe.wait_ge(turn_free, ph.turn + 2 * TT + s + 1)
                    out_tile(ph.unit + 12 + s, ((zT_hi, zT_lo), s), t, s == 0, halves)

                first_chunk(ph)
                project(ph, ph.unit + 4, 0, ph.group + 2, 0)
                project(ph, ph.unit + 4, 0, ph.group + 3, 1, fills={1: lambda: (turn_in(0), turn_in(1))})
                project(ph, ph.unit + 8, 0, ph.group + 4, 0,
                        fills={1: lambda: (turn_in(2), turn_in(3)), 2: lambda: scores(0), 3: lambda: scores(1)})
                project(ph, ph.unit + 8, 0, ph.group + 5, 1,
                        fills={2: lambda: turn_p(0), 3: lambda: values(0)})
                scores(2)
                turn_p(1)
                turn_in(4)
                turn_in(5)
                values(1)
                scores(3)
                out(0, 0)
                for s in range(2, pairs):
                    turn_p(s)
                    if s + 2 < pairs:
                        out(s - 2, 1)
                        values(s)
                        scores(s + 2)
                    else:
                        out(s - 2, 1, [0])
                        values(s)
                        out(s - 2, 1, [1])
                    if s + 1 < pairs:
                        out(s - 1, 0)
                out_last(ph, z_pair(pairs - 2), lambda: pe.wait_ge(turn_free, ph.turn + 2 * TT + pairs))

            def mlstm(ph):
                first_chunk(ph)

                def gates():
                    pe.wait_ge(gate_w, 1)
                    for k in range(KD):
                        pe.matmul(turn[:, 0, 0:SEQ], wg_hi[:, k, :], xT_hi[:, k, :], start=(k == 0), stop=False)
                        pe.matmul(turn[:, 0, 0:SEQ], wg_hi[:, k, :], xT_lo[:, k, :], start=False, stop=False)
                        pe.matmul(turn[:, 0, 0:SEQ], wg_lo[:, k, :], xT_hi[:, k, :], start=False, stop=(k == KD - 1))
                    pe.wait_ge(m_dready, 1)
                    pe.matmul(turn[:, 0, SEQ:2 * SEQ], const[:, C_ONE:C_ONE + P], m_diag, start=True,
                              stop=True).then_inc(m_gfull, 1)

                def turned_qk(b):
                    pe.wait_ge(proj_free, ph.group + 4)
                    for j in range(2):
                        for t in range(TT):
                            f = (2 * b + j) * P
                            last = pe.transpose(acc[:, b, j * SEQ + t * P:j * SEQ + (t + 1) * P],
                                                m_qk[:, t, f:f + P], ident)
                    last.then_inc(m_turned, 1)

                def gate_columns():
                    pe.wait_ge(m_rows, 1)
                    for j, src in enumerate((m_a, m_cm)):
                        for t in range(TT):
                            last = pe.transpose(turn[:, 0, (2 * j + t) * MH:(2 * j + t + 1) * MH],
                                                src[0:MH, t * P:(t + 1) * P], ident[0:MH, 0:MH])
                    last.then_inc(m_cfull, 1)

                def scores(h):
                    b, at, pair = h % 2, h % 2 * MDK, h // 2
                    if h == 0:
                        pe.wait_ge(m_tcopy, 4)
                    if h >= 2:
                        pe.wait_ge(m_pdone, h - 1)
                    for s in range(TT):
                        pe.matmul(acc[:, b, s * SEQ:s * SEQ + (TT - s) * P], m_kT[at:at + MDK, pair, s * P:(s + 1) * P],
                                  m_qT[at:at + MDK, pair, s * P:SEQ], start=True, stop=True)
                    pe.matmul(acc[:, 2 + b, 0:SEQ], sel[:, h * P:(h + 1) * P], M_hi[:, :], start=True, stop=False)
                    pe.matmul(acc[:, 2 + b, 0:SEQ], sel[:, h * P:(h + 1) * P], M_lo[:, :], start=False,
                              stop=True).then_inc(m_sfull, 1)

                def values(h):
                    pe.wait_ge(m_pdone, h + 1)
                    if h == 0:
                        pe.wait_ge(m_cols, 1)
                        pe.wait_ge(m_ones, 1)
                    if h >= 2:
                        pe.wait_ge(m_ycopy, h - 1)
                    if h % 4 == 0:
                        pe.wait_ge(proj_free, ph.group + 6 + h // 2)
                    for t in range(TT):
                        for s in range(t + 1):
                            last = pe.matmul(turn[:, h % 2, t * (MDV + 1):(t + 1) * (MDV + 1)],
                                             m_p[h % 2][:, (t + s) * P:(t + s + 1) * P], m_v[:, s * MH + h, :],
                                             start=(s == 0), stop=(s == t))
                    last.then_inc(m_yfull, 1)

                def turn_y(b):
                    pe.wait_ge(m_y, 2 * (b + 1))
                    if b >= 2:
                        pe.wait_ge(turn_free, ph.turn + 2 * TT + b - 1)
                    for j in range(2):
                        for t in range(TT):
                            f = (2 * b + j) * P
                            last = pe.transpose(turn[:, b % 2, j * SEQ + t * P:j * SEQ + (t + 1) * P],
                                                m_o[:, t, f:f + P], ident)
                    last.then_inc(turn_full, 1)

                fills = {-7: lambda: (turned_qk(0), turned_qk(1)),
                         -6: lambda: (turned_qk(2), turned_qk(3)), -4: gate_columns, -2: lambda: scores(0),
                         -1: lambda: scores(1), 22: lambda: turn_y(0), 23: lambda: turn_y(1)}
                for t in range(TT):
                    project(ph, ph.unit + 4, 0, ph.group + 2 + t, t, fills={0: gates} if t == 0 else {})
                for s, ch, place in m_quarters():
                    t, q = place // 4, place % 4
                    project(ph, ph.unit + 4 * ch, 0, ph.group + 2 * ch + t, t, [q])
                    if s in fills:
                        fills[s]()
                    h = m_head(s)
                    if h is not None:
                        values(h)
                        if h + 2 < MH:
                            scores(h + 2)

                mixer_out(ph, [z_pair(2 * b) for b in range(4)], {1: lambda: (turn_y(2), turn_y(3))})

            def ret(ph):
                def turned(h):
                    pe.wait_ge(r_rot, TT * (2 if h < 2 else 4))
                    for j in range(2):
                        for half in range(2):
                            for t in range(TT):
                                f = j * D + h * RDK
                                src = r_qkv[:, t, f:f + RDK].rearrange("p (e two) -> p two e", two=2)[:, half, :]
                                last = pe.transpose(acc[:, j, half * SEQ + t * P:half * SEQ + (t + 1) * P], src, ident)
                        last.then_inc(r_turned, 1)

                def scores(h):
                    pe.wait_ge(r_tcopy, 2 * (h + 1))
                    if h:
                        pe.wait_ge(r_norm, TT * h)
                    qT, kT = r_qk[h % 2][:, 0, :], r_qk[h % 2][:, 1, :]
                    for s in range(TT):
                        for half in range(2):
                            at = half * SEQ
                            last = pe.matmul(acc[:, 2, s * SEQ:s * SEQ + (TT - s) * P],
                                             kT[:, at + s * P:at + (s + 1) * P], qT[:, at + s * P:at + SEQ],
                                             start=(half == 0), stop=(half == 1))
                    last.then_inc(r_sfull, 1)

                def values(h, t):
                    if t == 0:
                        pe.wait_ge(r_pdone, h + 1)
                        pe.wait_ge(proj_free, ph.group + TT * (R_HEAD + h))
                    for s in range(t + 1):
                        last = pe.matmul(acc[:, 3 - t, :], r_p[h % 2][:, (t + s) * P:(t + s + 1) * P],
                                         r_qkv[:, s, 2048 + h * RDV:2048 + (h + 1) * RDV],
                                         start=(s == 0), stop=(s == t))
                    last.then_inc(r_yfull, 1)

                def turn_y(h):
                    pe.wait_ge(proj_free, ph.group + TT * (R_GATE + h + 1))
                    for b in range(2):
                        if h:
                            pe.wait_ge(turn_free, ph.turn + 2 * TT + 2 * h + b - 1)
                        for j in range(2):
                            for t in range(TT):
                                f = 2048 + h * RDV + (2 * b + j) * P
                                last = pe.transpose(turn[:, b, j * SEQ + t * P:j * SEQ + (t + 1) * P],
                                                    r_qkv[:, t, f:f + P], ident)
                        last.then_inc(turn_full, 1)

                first_chunk(ph)
                for ch in range(1, 12):
                    h, y = ch - R_HEAD, ch - R_GATE - 1
                    fills = {}
                    if 0 <= h < RH:
                        fills = {0: lambda: turned(h), 2: lambda: scores(h), 4: lambda: values(h, 0),
                                 5: lambda: values(h, 1)}
                    if y >= 0:
                        fills[1] = lambda: turn_y(y)
                    for t in range(TT):
                        project(ph, ph.unit + 4 * ch, 0, ph.group + 2 * ch + t, t,
                                fills={at - 4 * t: f for at, f in fills.items() if at // 4 == t})
                mixer_out(ph, [z_pair(2 * b) for b in range(4)] +
                          [[((xT_hi, xT_lo), 2 * b), ((xT_hi, xT_lo), 2 * b + 1)] for b in range(4)],
                          {1: lambda: turn_y(3)})

            pe.wait_ge(const_in, 16)
            turn_x(0, 0, 0)
            turn_x(0, 0, 1)
            pe.wait_ge(rows_in, 16)
            pe.wait_ge(own_rows_in, 32)
            pe.transpose(acc[:, 0, 0:ALL_ROWS], nw_rows[0:ALL_ROWS, :], ident[0:ALL_ROWS, 0:ALL_ROWS]) \
              .then_inc(nw_turned, 1)
            for ph in phases:
                {"ffn": ffn, "attn": attn, "mlstm": mlstm, "ret": ret}[ph.kind](ph)

        @block.scalar
        def _(act):
            def x_hi(ph, t, halves=range(2)):
                for half in halves:
                    act.wait_ge(turn_full, ph.turn + 2 * t + half + 1)
                    for k in range(4):
                        f = 4 * half + k
                        last = act.activation(xT_hi[:, f, t * P:(t + 1) * P], turn[:, half, k * P:(k + 1) * P],
                                              ACT.Copy, scale=nw[:, norm_col(ph) + f:norm_col(ph) + f + 1])
                    last.then_inc(turn_hi, 1)

            def squares(p, t):
                x_wait(act, p, t, 0)
                x_wait(act, p, t, 1)
                act.activation(acc[:, 2 * t:2 * t + 2, :].rearrange("p a b -> p (a b)"), xs[:, t, :], ACT.Square,
                               accum_out=ssq[:, t:t + 1]).then_inc(ssq_done, 1)

            def roots(p, first, last):
                act.wait_ge(ssq_done, TT * p + last + 1)
                act.activation(rms[:, first:last + 1], ssq[:, first:last + 1], ACT.Sqrt, scale=1.0 / D,
                               bias=eps[:, 0:1]).then_inc(rms_done, 1)

            def start(ph):
                if ph.n:
                    x_hi(ph, 0)
                squares(ph.n, 0)
                split_hi(act, ph.unit + 4)
                x_hi(ph, 1)
                split_hi(act, ph.unit + 5)
                squares(ph.n, 1)
                roots(ph.n, 0, TT - 1)

            def silu_gate(ph, c, t):
                projected(act, ph, c, t)
                act.activation(f_gate[:, t, :], proj[:, t, 0:CH], ACT.Silu, scale=rstd[:, t:t + 1]) \
                   .then_inc(gate_done, 1)

            def turned_hi(bank, k, threshold):
                act.wait_ge(turn_full, threshold)
                act.activation(zT_hi[:, k:k + 2, :].rearrange("p a b -> p (a b)"), turn[:, bank, :], ACT.Copy) \
                   .then_inc(turn_hi, 1)

            def ffn(ph, final):
                start(ph)
                act.wait_ge(rstd_ready, ph.n + 1)
                silu_gate(ph, 0, 0)
                for q in range(2, 4):
                    split_hi(act, ph.unit + 4 + q)
                silu_gate(ph, 0, 1)

                def chunk(c, ahead=(3, 1)):
                    n = ph.unit + 2
                    split_hi(act, n, c)
                    split_hi(act, n + 1, c)
                    turned_hi(0, 0, count(ph.turn + 2 * TT, c, 1))
                    silu_gate(ph, c, 0)
                    for q in range(ahead[0]):
                        split_hi(act, n + 2 + q, c)
                    silu_gate(ph, c, 1)
                    for q in range(ahead[1]):
                        split_hi(act, n + 2 + ahead[0] + q, c)

                chunk(1)
                with act.Fori(2, NCH - 1) as c:
                    chunk(c)
                if ph.n == 0:
                    act.wait_ge(angles_ready, 1)
                    for table, angle in ((sin, t_r), (cos, t_k)):
                        act.activation(table[:, :, :], angle, ACT.Sin).then_inc(sincos, 1)
                chunk(NCH - 1, (2, 0) if final else (2, 2))
                turned_hi(1, 2, ph.turn + 2 * TT + NCH)
                if not final:
                    split_hi(act, ph.unit + 6 * NCH + 2)
                    split_hi(act, ph.unit + 6 * NCH + 3)
                else:
                    act.activation(warm[:, 0:1], eps[:, 0:1], ACT.Sqrt)

            def attn(ph):
                i = ph.mixer
                pairs = HEADS // 2
                start(ph)

                def copy_in(b):
                    act.wait_ge(a_turned, 6 * i + b + 1)
                    dst = a_kT[:, 0:2, :] if b == 0 else a_qT[:, 2 * b - 4:2 * b - 2, :]
                    src = turn[:, b] if b < 2 else acc[:, 2 + b % 2]
                    act.activation(dst.rearrange("p a b -> p (a b)"), src, ACT.Copy).then_inc(a_evac_a, 1)

                def probabilities(s):
                    act.wait_ge(a_max, pairs * i + s + 1)
                    act.activation(a_se[:, s, :], a_se[:, s, :], ACT.Exp)
                    for t in range(TT):
                        for j in range(2):
                            p = a_s[s % 2][:, j, t * P:t * P + (t + 1) * P]
                            k = t * 2 + j
                            last = act.activation(p, p, ACT.Exp, bias=a_nm[:, s, k:k + 1],
                                                  accum_out=a_sum[:, s, k:k + 1])
                    last.then_inc(a_exp, 1)

                def split(first, n):
                    for q in range(n):
                        split_hi(act, ph.unit + first + q)

                def p_copy(s):
                    act.wait_ge(a_pfull, 2 * (pairs * i + s) + 1)
                    act.activation(a_pT[s % 2][:, 0:NB], turn[:, 0, :], ACT.Copy).then_inc(a_pcopy_a, 1)

                def z_hi(s):
                    act.wait_ge(turn_full, ph.turn + 2 * TT + s + 1)
                    act.activation(zT_hi[:, s, :], turn[:, 1, SEQ:2 * SEQ], ACT.Copy).then_inc(turn_hi, 1)

                split(6, 4)
                copy_in(0)
                split(10, 4)
                copy_in(2)
                probabilities(0)
                probabilities(1)
                p_copy(0)
                split(14, 1)
                z_hi(0)
                split(15, 1)
                p_copy(1)
                probabilities(2)
                copy_in(4)
                z_hi(1)
                split(16, 1)
                p_copy(2)
                probabilities(3)
                split(17, 1)
                for s in range(2, pairs):
                    z_hi(s)
                    if s + 1 < pairs:
                        p_copy(s + 1)
                    if s + 2 < pairs:
                        probabilities(s + 2)
                    split(16 + s, 1)

            def mlstm(ph):
                start(ph)

                def gates():
                    act.wait_ge(m_graw, 1)
                    for r in (slice(0, MH), slice(32, 32 + MH)):
                        last = act.activation(m_th[r, :], m_g[r, :], ACT.Tanh, scale=1 / CAP, bias=bgate[r, 1:2])
                    last.then_inc(m_act, 1)
                    act.wait_ge(m_act, 1)
                    act.activation(m_e[0:MH, :], m_th[32:32 + MH, :], ACT.Exp, scale=-CAP).then_inc(m_act, 1)
                    act.wait_ge(m_act, 2)
                    act.activation(m_nl[0:MH, :], m_e[0:MH, :], ACT.Ln, bias=1.0).then_inc(m_act, 1)

                def turned_qk():
                    for b in range(4):
                        act.wait_ge(m_turned, b + 1)
                        dst = m_qT[:, 2 * b:2 * b + 2, :] if b < 2 else m_kT[:, 2 * b - 4:2 * b - 2, :]
                        act.activation(dst.rearrange("p a b -> p (a b)"), acc[:, b, :], ACT.Copy,
                                       scale=MDK ** -0.5 if b < 2 else 1.0).then_inc(m_tcopy, 1)

                def row_exp():
                    act.wait_ge(m_cfull, 1)
                    act.activation(m_em[:, :, :].rearrange("p a b -> p (a b)"), turn[:, 0, 2 * MH:4 * MH], ACT.Exp) \
                       .then_inc(m_emd, 1)

                def weights(h):
                    act.wait_ge(m_wpre, h + 1)
                    act.wait_ge(m_cols, 1)
                    w = m_w[h % 2]
                    act.activation(w[:, 0:SEQ], w[:, 0:SEQ], ACT.Exp, bias=m_acol[:, 0, h:h + 1])
                    act.activation(w[:, SEQ:TRI], w[:, SEQ:TRI], ACT.Exp, bias=m_acol[:, 1, h:h + 1]) \
                       .then_inc(m_wexp, 1)

                def squares(h):
                    act.wait_ge(m_yfull, h + 1)
                    if h:
                        act.wait_ge(m_ssd, h)
                    for t in range(TT):
                        y = turn[:, h % 2, t * (MDV + 1):t * (MDV + 1) + MDV]
                        last = act.activation(m_sq[:, t, :], y, ACT.Square, accum_out=m_ss[:, t, h:h + 1])
                    last.then_inc(m_ssd, 1)

                def sigmoid(half):
                    act.wait_ge(proj_free, ph.group + 10 + 2 * half)
                    o = m_o[:, :, half * NB:(half + 1) * NB]
                    act.activation(o, o, ACT.Sigmoid).then_inc(m_sig, 1)

                def root_var():
                    act.wait_ge(m_var, 1)
                    act.activation(m_rs[:, :, :], m_t[:, :, :], ACT.Sqrt, scale=1 / MDV, bias=eps[:, 0:1]) \
                       .then_inc(m_root, 1)

                def z_hi(b):
                    act.wait_ge(turn_full, ph.turn + 2 * TT + b + 1)
                    for j in range(2):
                        k = 2 * b + j
                        last = act.activation(zT_hi[:, k, :], turn[:, b % 2, j * SEQ:(j + 1) * SEQ], ACT.Copy,
                                              scale=nw[:, N_ROWS + k:N_ROWS + k + 1])
                    last.then_inc(turn_hi, 1)

                for q in range(2, 4):
                    split_hi(act, ph.unit + 4 + q)
                for q in range(4):
                    if q == 2:
                        gates()
                    split_hi(act, ph.unit + 8 + q)
                steps = {-6: turned_qk, -4: row_exp, -2: lambda: weights(0), -1: lambda: weights(1),
                         16: lambda: sigmoid(0), 17: root_var, 22: lambda: z_hi(0), 23: lambda: z_hi(1)}
                for s, ch, place in m_quarters():
                    if s in steps:
                        steps[s]()
                    h = m_head(s)
                    if h is not None:
                        squares(h)
                        if h + 2 < MH:
                            weights(h + 2)
                    split_ahead(split_hi, act, ph, ch, place)
                sigmoid(1)
                for q in range(4):
                    split_hi(act, ph.unit + 28 + q)
                z_hi(2)
                z_hi(3)
                for q in range(4):
                    split_hi(act, ph.unit + 32 + q)

            def ret(ph):
                start(ph)

                def turned(h):
                    for j in range(2):
                        act.wait_ge(r_turned, 2 * h + j + 1)
                        act.activation(r_qk[h % 2][:, j, :], acc[:, j, :], ACT.Copy).then_inc(r_tcopy, 1)

                def deviations(h):
                    for t in range(TT):
                        n = TT * h + t
                        act.wait_ge(r_mvd, n + 1)
                        act.activation(r_sd[:, n, :], r_mv[:, n, 1:2], ACT.Sqrt, bias=eps[:, 0:1]).then_inc(r_sdd, 1)

                def silu(ch, t):
                    projected(act, ph, ch, t)
                    if ch > R_GATE:
                        act.wait_ge(proj_free, ph.group + TT * (ch - 1) + t + 1)
                    act.activation(r_gate[:, t, :], proj[:, t, :], ACT.Silu, scale=rstd[:, t:t + 1]) \
                       .then_inc(r_silu, 1)

                def z_hi(h):
                    for b in range(2):
                        act.wait_ge(turn_full, ph.turn + 2 * TT + 2 * h + b + 1)
                        for j in range(2):
                            k = 4 * h + 2 * b + j
                            dst = zT_hi if k < KD else xT_hi
                            last = act.activation(dst[:, k % KD, :], turn[:, b, j * SEQ:(j + 1) * SEQ], ACT.Copy,
                                                  scale=nw[:, N_ROWS + KD + k:N_ROWS + KD + k + 1])
                        last.then_inc(turn_hi, 1)

                for q in range(2, 4):
                    split_hi(act, ph.unit + 4 + q)
                for ch in range(1, 12):
                    h, y = ch - R_HEAD, ch - R_GATE - 1
                    for place in range(8):
                        if ch >= R_GATE and place % 4 == 3:
                            silu(ch, place // 4)
                        if 0 <= h < RH and place == 0:
                            turned(h)
                        if 0 <= y < RH - 2 and place == 1:
                            z_hi(y)
                        split_ahead(split_hi, act, ph, ch, place)
                        if 0 <= h < RH and place == 6:
                            deviations(h)
                split_hi(act, ph.unit + 52)
                z_hi(2)
                split_hi(act, ph.unit + 53)
                for i in range(KOUT["ret"] - 2):
                    split_hi(act, ph.unit + 54 + i)
                    if i == 1:
                        z_hi(3)

            act.dma_start(ident, consts[:, C_ID:C_ID + P]).then_inc(const_in, 16)
            act.dma_start(nw_rows[0:N_ROWS, :], norm_w.rearrange("l w (k f) -> (l w k) f", f=P)).then_inc(rows_in, 16)
            split_hi(act, 0)
            act.wait_ge(nw_ready, 1)
            x_hi(phases[0], 0, [0])
            split_hi(act, 1)
            x_hi(phases[0], 0, [1])
            for n in (2, 3):
                split_hi(act, n)
            act.wait_ge(eps_set, 1)
            for ph in phases:
                if ph.kind == "ffn":
                    ffn(ph, ph.n == len(phases) - 1)
                else:
                    {"attn": attn, "mlstm": mlstm, "ret": ret}[ph.kind](ph)
            for t in range(TT):
                squares(len(phases), t)
                roots(len(phases), t, t)

        @block.vector
        def _(v):
            chain = [0]

            def link(ins):
                chain[0] += 1
                ins.then_inc(dve, 1)
                v.wait_ge(dve, chain[0])

            def x_lo(ph, t, halves=range(2)):
                for half in halves:
                    v.wait_ge(turn_hi, ph.turn + 2 * t + half + 1)
                    for k in range(4):
                        f = 4 * half + k
                        last = v.scalar_tensor_tensor(xT_lo[:, f, t * P:(t + 1) * P], turn[:, half, k * P:(k + 1) * P],
                                                      nw[:, norm_col(ph) + f:norm_col(ph) + f + 1],
                                                      xT_hi[:, f, t * P:(t + 1) * P].bitcast(F32),
                                                      ALU.mult, ALU.subtract)
                    last.then_inc(turn_free, 1)

            def inverse(p, first, last):
                n = p + first + 1 if p == len(phases) else p + 1
                v.wait_ge(rms_done, n)
                v.reciprocal(rstd[:, first:last + 1], rms[:, first:last + 1]).then_inc(rstd_ready, 1)

            def add_x(ph, t, half):
                accumulated(v, ph, t, half)
                xq = xs[:, t, half * NB:(half + 1) * NB]
                v.scalar_tensor_tensor(xq, acc[:, 2 * t + half, :], 0.5 if ph.kind == "ffn" else 1.0, xq,
                                       ALU.mult, ALU.add).then_inc(x_ready, 1)

            def after_turns(ph):
                split_lo(v, ph.unit + 4)
                x_lo(ph, 1)
                split_lo(v, ph.unit + 5)
                inverse(ph.n, 0, TT - 1)

            def finish(ph):
                add_x(ph, 0, 0)
                add_x(ph, 0, 1)
                if ph.n + 1 == len(phases):
                    last_norm(ph)
                    return
                following = phases[ph.n + 1]
                split_lo(v, following.unit + 3)
                x_lo(following, 0, [0])
                add_x(ph, 1, 0)
                x_lo(following, 0, [1])
                add_x(ph, 1, 1)
                after_turns(following)

            def last_norm(ph):
                def quarter(t, half):
                    x_ = xs[:, t, half * NB:(half + 1) * NB]
                    v.scalar_tensor_tensor(x_, x_, rstd[:, t:t + 1], final_w[:, half * NB:(half + 1) * NB],
                                           ALU.mult, ALU.mult).then_inc(out_ready, 1)

                add_x(ph, 1, 0)
                v.wait_ge(final_in, 16)
                for t in range(TT):
                    inverse(len(phases), t, t)
                    v.wait_ge(rstd_ready, len(phases) + t + 1)
                    if t == 0:
                        add_x(ph, 1, 1)
                    quarter(t, 0)
                    quarter(t, 1)

            def hidden(ph, c, t):
                v.wait_ge(gate_done, count(TT * NCH * ph.ffn + t + 1, c, TT))
                v.scalar_tensor_tensor(f_hid[:, t, :], proj[:, t, CH:2 * CH], rstd[:, t:t + 1], f_gate[:, t, :],
                                       ALU.mult, ALU.mult).then_inc(proj_free, 1)

            def turned_lo(bank, k, threshold):
                v.wait_ge(turn_hi, threshold)
                v.tensor_tensor(zT_lo[:, k:k + 2, :].rearrange("p a b -> p (a b)"), turn[:, bank, :],
                                zT_hi[:, k:k + 2, :].rearrange("p a b -> p (a b)").bitcast(F32), ALU.subtract) \
                 .then_inc(turn_free, 1)

            def ffn(ph, final):
                v.wait_ge(rstd_ready, ph.n + 1)
                hidden(ph, 0, 0)
                for q in range(2, 4):
                    split_lo(v, ph.unit + 4 + q)
                hidden(ph, 0, 1)

                def chunk(c, ahead=(3, 1)):
                    n = ph.unit + 2
                    split_lo(v, n, c)
                    split_lo(v, n + 1, c)
                    turned_lo(0, 0, count(ph.turn + 2 * TT, c, 1))
                    hidden(ph, c, 0)
                    for q in range(ahead[0]):
                        split_lo(v, n + 2 + q, c)
                    hidden(ph, c, 1)
                    for q in range(ahead[1]):
                        split_lo(v, n + 2 + ahead[0] + q, c)

                chunk(1)
                with v.Fori(2, NCH - 1) as c:
                    chunk(c)
                chunk(NCH - 1, (2, 0) if final else (2, 2))
                turned_lo(1, 2, ph.turn + 2 * TT + NCH)
                if not final:
                    split_lo(v, ph.unit + 6 * NCH + 2)
                finish(ph)

            def attn(ph):
                i = ph.mixer
                pairs = HEADS // 2

                def copy_in(b):
                    v.wait_ge(a_turned, 6 * i + b + 1)
                    dst = a_kT[:, 2:4, :] if b == 1 else a_qT[:, 2 * b - 4:2 * b - 2, :]
                    src = turn[:, b] if b < 2 else acc[:, 2 + b % 2]
                    v.tensor_copy(dst.rearrange("p a b -> p (a b)"), src).then_inc(a_evac_v, 1)

                def maxima(s):
                    v.wait_ge(a_sfull, pairs * i + s + 1)
                    bank = acc[:, s % 2 * 2:s % 2 * 2 + 2, :] if s < 3 else proj
                    for t in range(TT):
                        for j in range(2):
                            cols = slice(t * P, t * P + (t + 1) * P)
                            last = v.tensor_tensor_reduce(a_s[s % 2][:, j, cols], bank[:, j, cols],
                                                          const[:, C_MA + t * P:C_MA + t * P + (t + 1) * P],
                                                          HD ** -0.5, -3e38, ALU.add, ALU.max,
                                                          a_mx[:, s, t * 2 + j:t * 2 + j + 1])
                    last.then_inc(a_masked, 1)
                    v.wait_ge(a_masked, pairs * i + s + 1)
                    two = "p (t h) -> p t h"
                    ns = a_nsink[:, 2 * s:2 * s + 2].rearrange("p (o h) -> p o h", o=1).to_broadcast([P, TT, 2])
                    sk = sinks[:, i:i + 1, 2 * s:2 * s + 2].to_broadcast([P, TT, 2])
                    link(v.scalar_tensor_tensor(a_nm[:, s, :].rearrange(two, t=TT), a_mx[:, s, :].rearrange(two, t=TT),
                                                -1.0, ns, ALU.mult, ALU.min))
                    v.tensor_tensor(a_se[:, s, :].rearrange(two, t=TT), a_nm[:, s, :].rearrange(two, t=TT), sk,
                                    ALU.add).then_inc(a_max, 1)

                def evacuate(ch, t):
                    at = COLUMNS["attn"][ch] * NB
                    return v.scalar_tensor_tensor(a_qkv[:, t, at:at + NB], proj[:, t, :], rstd[:, t:t + 1],
                                                  a_bias[:, at:at + NB], ALU.mult, ALU.add)

                v.wait_ge(rstd_ready, ph.n + 1)
                v.wait_ge(bias_in, 32 * (i + 1))
                v.wait_ge(nsink, i + 1)
                def chunk(ch, t):
                    projected(v, ph, ch, t)
                    evacuate(ch, t).then_inc(proj_free, 1)

                def split(first, n):
                    for q in range(n):
                        split_lo(v, ph.unit + first + q)

                def p_copy(s):
                    v.wait_ge(a_pfull, 2 * (pairs * i + s) + 2)
                    v.tensor_copy(a_pT[s % 2][:, NB:NB + SEQ], turn[:, 1, 0:SEQ]).then_inc(a_pcopy_v, 1)

                def normed(s):
                    v.wait_ge(a_exp, pairs * i + s + 1)
                    link(v.tensor_tensor(a_den[:, s, :], a_sum[:, s, :], a_se[:, s, :], ALU.add))
                    link(v.reciprocal(a_rden[:, s, :], a_den[:, s, :]))
                    for t in range(TT):
                        for j in range(2):
                            p = a_s[s % 2][:, j, t * P:t * P + (t + 1) * P]
                            last = v.tensor_scalar(p, p, a_rden[:, s, t * 2 + j:t * 2 + j + 1], None, ALU.mult)
                    last.then_inc(a_normed, 1)

                def z_lo(s):
                    v.wait_ge(turn_hi, ph.turn + 2 * TT + s + 1)
                    v.tensor_tensor(zT_lo[:, s, :], turn[:, 1, SEQ:2 * SEQ], zT_hi[:, s, :].bitcast(F32), ALU.subtract) \
                     .then_inc(turn_free, 1)

                chunk(0, 0)
                split(6, 1)
                chunk(0, 1)
                split(7, 1)
                chunk(1, 0)
                split(8, 2)
                copy_in(1)
                split(10, 1)
                chunk(1, 1)
                split(11, 1)
                copy_in(3)
                maxima(0)
                chunk(2, 0)
                maxima(1)
                normed(0)
                split(12, 2)
                normed(1)
                p_copy(0)
                split(14, 1)
                chunk(2, 1)
                z_lo(0)
                maxima(2)
                p_copy(1)
                split(15, 1)
                copy_in(5)
                normed(2)
                z_lo(1)
                maxima(3)
                for s in range(2, pairs):
                    p_copy(s)
                    split(14 + s if s < pairs - 1 else 15 + s, 1)
                    if s + 1 < pairs:
                        normed(s + 1)
                    z_lo(s)
                    if s + 2 < pairs:
                        maxima(s + 2)
                    if s == pairs - 2:
                        split(15 + s, 1)
                v.wait_ge(bo_added, i + 1)
                finish(ph)

            def mlstm(ph):
                def evacuate(ch, t):
                    r = rstd[:, t:t + 1]
                    if ch < 2:
                        return v.tensor_scalar(m_qk[:, t, ch * NB:(ch + 1) * NB], proj[:, t, :], r, None, ALU.mult)
                    if ch < 4:
                        h = t * MH + 4 * (ch - 2)
                        return v.tensor_scalar(m_v[:, h:h + 4, 0:MDV], proj[:, t, :].rearrange("p (h e) -> p h e", h=4),
                                               r, None, ALU.mult)
                    return v.tensor_scalar(m_o[:, t, (ch - 4) * NB:(ch - 3) * NB], proj[:, t, :], r, None, ALU.mult)

                def diagonals():
                    for t in range(TT):
                        last = v.tensor_scalar(m_diag[:, t * P:(t + 1) * P], ident, rstd[:, t:t + 1], None, ALU.mult)
                    last.then_inc(m_dready, 1)

                def gates():
                    r = slice(0, 32 + MH)
                    v.wait_ge(m_gfull, 1)
                    link(v.tensor_copy(m_R[r, :], turn[r, 0, SEQ:2 * SEQ]))
                    v.tensor_tensor(m_g[r, :], turn[r, 0, 0:SEQ], m_R[r, :], ALU.mult).then_inc(m_graw, 1)

                def rows():
                    v.wait_ge(m_act, 3)
                    r = slice(0, MH)
                    link(v.tensor_tensor_scan(m_C[r, :], const[r, C_ONE:C_ONE + SEQ], m_nl[r, :], 0.0,
                                              ALU.mult, ALU.add))
                    link(v.scalar_tensor_tensor(m_a[r, :], m_th[r, :], CAP, m_C[r, :], ALU.mult, ALU.add))
                    link(v.tensor_tensor_scan(m_M[r, :], m_a[r, :], m_a[r, :], 0.0, ALU.max, ALU.max))
                    link(v.tensor_copy(M_hi[:, :], m_M[r, :]))
                    v.tensor_tensor(M_lo[:, :], m_M[r, :], M_hi[:, :].bitcast(F32), ALU.subtract)
                    v.tensor_tensor(m_cm[r, :], m_C[r, :], m_M[r, :], ALU.subtract).then_inc(m_rows, 1)

                def columns():
                    v.wait_ge(m_emd, 1)
                    v.tensor_copy(m_acol[:, :, :].rearrange("p a b -> p (a b)"), turn[:, 0, 0:2 * MH]) \
                     .then_inc(m_cols, 1)

                def shifted(h):
                    v.wait_ge(m_sfull, h + 1)
                    v.tensor_tensor(m_w[h % 2][:, 0:SEQ], const[:, C_MB:C_MB + SEQ], acc[:, 2 + h % 2, 0:SEQ],
                                    ALU.subtract)
                    v.tensor_tensor(m_w[h % 2][:, SEQ:TRI], const[:, C_MB + SEQ:C_MB + TRI], acc[:, 2 + h % 2, P:SEQ],
                                    ALU.subtract).then_inc(m_wpre, 1)

                def weighted(h):
                    v.wait_ge(m_wexp, h + 1)
                    v.tensor_tensor(m_p[h % 2], acc[:, h % 2, 0:TRI], m_w[h % 2], ALU.mult).then_inc(m_pdone, 1)

                def copies(h):
                    v.wait_ge(m_ssd, h + 1)
                    v.tensor_copy(m_num[:, TT * h:TT * (h + 1), :].rearrange("p a b -> p (a b)"),
                                  turn[:, h % 2, 0:TT * (MDV + 1)]).then_inc(m_ycopy, 1)

                def variances():
                    v.wait_ge(m_ycopy, MH)
                    nq = m_num[:, :, MDV].rearrange("p (h t) -> p t h", t=TT)
                    link(v.scalar_tensor_tensor(m_den[:, :, :], nq, -1.0, nq, ALU.mult, ALU.max))
                    link(v.tensor_tensor(m_den[:, :, :], m_den[:, :, :], m_em[:, :, :], ALU.max))
                    link(v.reciprocal(m_rd[:, :, :], m_den[:, :, :]))
                    link(v.tensor_tensor(m_t[:, :, :], m_ss[:, :, :], m_rd[:, :, :], ALU.mult))
                    v.tensor_tensor(m_t[:, :, :], m_t[:, :, :], m_rd[:, :, :], ALU.mult).then_inc(m_var, 1)

                def factors():
                    v.wait_ge(m_root, 1)
                    link(v.reciprocal(m_fs[:, :, :], m_rs[:, :, :]))
                    link(v.tensor_tensor(m_fs[:, :, :], m_fs[:, :, :], m_rd[:, :, :], ALU.mult))

                def gated(heads):
                    v.wait_ge(m_sig, 1 + heads[0] // 4)
                    for h in heads:
                        for t in range(TT):
                            o = m_o[:, t, h * MDV:(h + 1) * MDV]
                            last = v.scalar_tensor_tensor(o, m_num[:, TT * h + t, 0:MDV], m_fs[:, t, h:h + 1], o,
                                                          ALU.mult, ALU.mult)
                        last.then_inc(m_y, 1)

                def z_lo(b):
                    v.wait_ge(turn_hi, ph.turn + 2 * TT + b + 1)
                    for j in range(2):
                        k = 2 * b + j
                        last = v.scalar_tensor_tensor(zT_lo[:, k, :], turn[:, b % 2, j * SEQ:(j + 1) * SEQ],
                                                      nw[:, N_ROWS + k:N_ROWS + k + 1], zT_hi[:, k, :].bitcast(F32),
                                                      ALU.mult, ALU.subtract)
                    last.then_inc(turn_free, 1)

                v.wait_ge(rstd_ready, ph.n + 1)
                diagonals()
                for ch in range(M_FROM):
                    for t in range(TT):
                        projected(v, ph, ch, t)
                        evacuate(ch, t).then_inc(proj_free, 1)
                        if ch == 1 and t == 0:
                            gates()
                        for q in (range(2 if ch == 0 else 0, 3), [3])[t]:
                            split_lo(v, ph.unit + 4 * (ch + 1) + q)
                steps = {-7: rows, -4: columns, -2: lambda: (shifted(0), weighted(0)), -1: lambda: shifted(1),
                         16: variances, 17: factors, 18: lambda: gated((0, 1)),
                         19: lambda: gated((2, 3)), 22: lambda: z_lo(0), 23: lambda: z_lo(1)}
                for s, ch, place in m_quarters():
                    if place % 4 == 3:
                        projected(v, ph, ch, place // 4)
                        evacuate(ch, place // 4).then_inc(proj_free, 1)
                    if s in steps:
                        steps[s]()
                    h = m_head(s)
                    if h is not None:
                        if h + 1 < MH:
                            weighted(h + 1)
                        if h + 2 < MH:
                            shifted(h + 2)
                        copies(h)
                    split_ahead(split_lo, v, ph, ch, place)
                split_lo(v, ph.unit + 28)
                gated((4, 5))
                gated((6, 7))
                for q in range(3):
                    split_lo(v, ph.unit + 29 + q)
                z_lo(2)
                z_lo(3)
                for q in range(3):
                    split_lo(v, ph.unit + 32 + q)
                finish(ph)

            def ret(ph):
                def evacuate(ch, t):
                    at = COLUMNS["ret"][ch] * NB
                    if ch < R_GATE:
                        projected(v, ph, ch, t)
                        ins = v.tensor_scalar(r_qkv[:, t, at:at + NB], proj[:, t, :], rstd[:, t:t + 1], None, ALU.mult)
                    else:
                        v.wait_ge(r_silu, TT * (ch - R_GATE) + t + 1)
                        y = r_qkv[:, t, at - 2048:at - 2048 + NB]
                        ins = v.tensor_tensor(y, y, r_gate[:, t, :], ALU.mult)
                    ins.then_inc(proj_free, 1)

                def rotate(ch, t):
                    v.wait_ge(proj_free, ph.group + 2 * ch + t + 1)
                    at = COLUMNS["ret"][ch] * NB
                    x_ = r_qkv[:, t, at:at + NB].rearrange("p (h e two) -> p h two e", h=2, two=2)
                    x1, x2 = x_[:, :, 0, :], x_[:, :, 1, :]
                    co = cos[:, t:t + 1, ROPE_HALF:N_INV].to_broadcast([P, 2, P])
                    si = sin[:, t:t + 1, ROPE_HALF:N_INV].to_broadcast([P, 2, P])
                    tm = [r_tmp[:, j, :].rearrange("p (h e) -> p h e", h=2) for j in range(4)]
                    v.tensor_tensor(tm[0], x1, co, ALU.mult)
                    v.tensor_tensor(tm[1], x2, si, ALU.mult)
                    v.tensor_tensor(tm[2], x2, co, ALU.mult)
                    link(v.tensor_tensor(tm[3], x1, si, ALU.mult))
                    v.tensor_tensor(x1, tm[0], tm[1], ALU.subtract)
                    v.tensor_tensor(x2, tm[2], tm[3], ALU.add).then_inc(r_rot, 1)
                    v.wait_ge(r_rot, TT * ch + t + 1)

                def decayed(h):
                    v.wait_ge(r_sfull, h + 1)
                    v.tensor_tensor(r_p[h % 2], acc[:, 2, 0:TRI], const[:, C_DM + h * TRI:C_DM + (h + 1) * TRI],
                                    ALU.mult).then_inc(r_pdone, 1)

                def moments(h):
                    for t in range(TT):
                        n = TT * h + t
                        v.wait_ge(r_yfull, n + 1)
                        link(v.bn_stats(r_bn[:, n, :], acc[:, 3 - t, :]))
                        v.bn_aggr(r_mv[:, n, :], r_bn[:, n, :]).then_inc(r_mvd, 1)

                def normed(h):
                    for t in range(TT):
                        n = TT * h + t
                        v.wait_ge(r_sdd, n + 1)
                        link(v.reciprocal(r_rs[:, n, :], r_sd[:, n, :]))
                        at = 2048 + h * RDV
                        v.tensor_scalar(r_qkv[:, t, at:at + RDV], acc[:, 3 - t, :], r_mv[:, n, 0:1], r_rs[:, n, :],
                                        ALU.subtract, ALU.mult).then_inc(r_norm, 1)

                def z_lo(h):
                    for b in range(2):
                        v.wait_ge(turn_hi, ph.turn + 2 * TT + 2 * h + b + 1)
                        for j in range(2):
                            k = 4 * h + 2 * b + j
                            hi, dst = (zT_hi, zT_lo) if k < KD else (xT_hi, xT_lo)
                            last = v.scalar_tensor_tensor(dst[:, k % KD, :], turn[:, b, j * SEQ:(j + 1) * SEQ],
                                                          nw[:, N_ROWS + KD + k:N_ROWS + KD + k + 1], hi[:, k % KD, :].bitcast(F32),
                                                          ALU.mult, ALU.subtract)
                        last.then_inc(turn_free, 1)

                v.wait_ge(rstd_ready, ph.n + 1)
                for t in range(TT):
                    evacuate(0, t)
                    split_lo(v, ph.unit + 6 + t)
                for ch in range(1, 12):
                    h, y, rot = ch - R_HEAD, ch - R_GATE - 1, ch - 2
                    for place in range(8):
                        if place % 4 == 3:
                            evacuate(ch, place // 4)
                        if 0 <= rot < 4 and place in (1, 4):
                            rotate(rot, place // 4)
                        if 0 <= y < RH - 2 and place == 1:
                            z_lo(y)
                        split_ahead(split_lo, v, ph, ch, place)
                        if 0 <= h < RH and place in (2, 6, 7):
                            {2: decayed, 6: moments, 7: normed}[place](h)
                split_lo(v, ph.unit + 52)
                z_lo(2)
                split_lo(v, ph.unit + 53)
                for i in range(KOUT["ret"] - 3):
                    split_lo(v, ph.unit + 54 + i)
                    if i == 1:
                        z_lo(3)
                finish(ph)

            v.wait_ge(nw_turned, 1)
            v.tensor_copy(nw[:, 0:ALL_ROWS], acc[:, 0, 0:ALL_ROWS]).then_inc(nw_ready, 1)
            v.wait_ge(nw_ready, 1)
            split_lo(v, 0)
            x_lo(phases[0], 0, [0])
            split_lo(v, 1)
            x_lo(phases[0], 0, [1])
            for n in (2, 3):
                split_lo(v, n)
            after_turns(phases[0])
            for ph in phases:
                if ph.kind == "ffn":
                    ffn(ph, ph.n == len(phases) - 1)
                else:
                    {"attn": attn, "mlstm": mlstm, "ret": ret}[ph.kind](ph)


_INS = ['x', 'positions', 'norm_w', 'final_norm_w', 'ffn_w_in', 'ffn_w_out', 'attn_w_qkv', 'attn_b_qkv', 'attn_w_o',
        'attn_b_o', 'attn_sinks', 'mlstm_w_in', 'mlstm_b_if', 'mlstm_norm_w', 'mlstm_w_out', 'ret_w_in', 'ret_norm_w',
        'ret_w_out']


def kernel(**inputs):
    import concourse.bacc as _bacc
    from concourse.bass_utils import run_bass_kernel_spmd as _run

    nc = _bacc.Bacc("TRN2", target_bir_lowering=False, num_devices=1)
    arrays, args = {}, []
    given = {name: np.ascontiguousarray(inputs[name]) for name in _INS}
    given["consts"] = constants()
    for name, a in given.items():
        arrays[f"in_{name}"] = a
        args.append(nc.dram_tensor(f"in_{name}", a.shape, mybir.dt.from_np(a.dtype), kind="ExternalInput").ap())
    args.append(nc.dram_tensor("out_0", (1, SEQ, D), F32, kind="ExternalOutput").ap())
    build(nc, *args)
    r = _run(nc, [arrays], core_ids=[0])
    return r.results[0]["out_0"]
```
